# Optimizing a Trainium2 kernel written in Bass

```python
import jax, jax.numpy as jnp
from jax import lax
import numpy as np
import math

D_MODEL = 1024
BATCH = 1
SEQ = 512
DEPTH = 1

MIX_WIDTH = D_MODEL
POOL_WIDTH = D_MODEL // 4
POOL_WINDOWS = (2, 4, 8, 16)
POOL_GROUP = POOL_WIDTH // len(POOL_WINDOWS)
HEAD_DIM = 64
ATTN_WIDTH = MIX_WIDTH - POOL_WIDTH
N_HEADS = ATTN_WIDTH // HEAD_DIM
DILATED_CONFIGS = ((128, 1), (512, 4), (2048, 16))
BLOCK = 128
ROPE_THETA = 10000.0
IN_WIDTH = POOL_WIDTH + 3 * ATTN_WIDTH
_FF_RAW = -(-8 * D_MODEL // 3)
D_FF = ((_FF_RAW + 255) // 256) * 256
EPS = 1e-6


def rms_norm(x, g):
    xf = x.astype(jnp.float32)
    y = xf * lax.rsqrt(jnp.mean(xf * xf, axis=-1, keepdims=True) + EPS)
    return (y * g.astype(jnp.float32)).astype(x.dtype)

def rope(x, pos):
    half = x.shape[-1] // 2
    freqs = ROPE_THETA ** (-jnp.arange(half, dtype=jnp.float32) * (2.0 / x.shape[-1]))
    ang = pos.astype(jnp.float32)[:, None] * freqs[None, :]
    cos = jnp.cos(ang)[None, :, None, :]
    sin = jnp.sin(ang)[None, :, None, :]
    xf = x.astype(jnp.float32)
    x1, x2 = xf[..., :half], xf[..., half:]
    out = jnp.concatenate([x1 * cos - x2 * sin, x2 * cos + x1 * sin], axis=-1)
    return out.astype(x.dtype)

def multi_scale_pool(u, w_pool, pool_scale):
    B, S, _ = u.shape
    ug = u.astype(jnp.float32).reshape(B, S, len(POOL_WINDOWS), POOL_GROUP)
    csum = lax.cumsum(ug, axis=1)
    t = jnp.arange(S)
    outs = []
    for gi, win in enumerate(POOL_WINDOWS):
        cg = csum[:, :, gi]
        shifted = jnp.pad(cg, ((0, 0), (win, 0), (0, 0)))[:, :S]
        cnt = jnp.minimum(t + 1, win).astype(jnp.float32)[None, :, None]
        outs.append((cg - shifted) / cnt - ug[:, :, gi])
    d = jnp.stack(outs, axis=2)
    y = jnp.einsum('bsgc,gcd->bsgd', d, w_pool.astype(jnp.float32))
    y = y.reshape(B, S, POOL_WIDTH) * pool_scale.astype(jnp.float32)
    return y.astype(u.dtype)

def dilated_branch(q, k, v, window, dilation):
    B, S, H, Dh = q.shape
    L = S // dilation
    nb = -(-L // BLOCK)
    Lp = nb * BLOCK
    w_sub = window // dilation

    def to_sub(a):
        a = a.reshape(B, L, dilation, H, Dh).transpose(0, 2, 1, 3, 4)
        return jnp.pad(a, ((0, 0), (0, 0), (0, Lp - L), (0, 0), (0, 0)))

    qs = to_sub(q).reshape(B, dilation, nb, BLOCK, H, Dh)
    kp = jnp.pad(to_sub(k), ((0, 0), (0, 0), (BLOCK, 0), (0, 0), (0, 0)))
    vp = jnp.pad(to_sub(v), ((0, 0), (0, 0), (BLOCK, 0), (0, 0), (0, 0)))

    def band(a):
        prev = a[:, :, :Lp].reshape(B, dilation, nb, BLOCK, H, Dh)
        cur = a[:, :, BLOCK:].reshape(B, dilation, nb, BLOCK, H, Dh)
        return jnp.concatenate([prev, cur], axis=3)

    kb, vb = band(kp), band(vp)
    scale = 1.0 / np.sqrt(Dh).astype(np.float32)
    s = jnp.einsum('brnqhd,brnkhd->brnhqk', qs.astype(jnp.float32), kb.astype(jnp.float32)) * scale

    qi = jnp.arange(BLOCK)[:, None]
    kj = jnp.arange(2 * BLOCK)[None, :]
    dist = qi + BLOCK - kj
    blk = jnp.arange(nb)[:, None, None]
    valid = (dist >= 0) & (dist <= w_sub) & (blk * BLOCK + kj - BLOCK >= 0)
    s = jnp.where(valid[None, None, :, None], s, -jnp.inf)

    m = jnp.max(s, axis=-1, keepdims=True)
    e = jnp.exp(s - m)
    den = jnp.sum(e, axis=-1, keepdims=True)
    lse = (m + jnp.log(den))[..., 0]
    o = jnp.einsum('brnhqk,brnkhd->brnqhd', e / den, vb.astype(jnp.float32))

    o = o.reshape(B, dilation, Lp, H, Dh)[:, :, :L].transpose(0, 2, 1, 3, 4).reshape(B, S, H, Dh)
    lse = lse.transpose(0, 1, 2, 4, 3).reshape(B, dilation, Lp, H)[:, :, :L]
    lse = lse.transpose(0, 2, 1, 3).reshape(B, S, H)
    return o, lse

def dilated_attention(q, k, v):
    outs, lses = [], []
    for window, dilation in DILATED_CONFIGS:
        o, lse = dilated_branch(q, k, v, window, dilation)
        outs.append(o)
        lses.append(lse)
    w = jax.nn.softmax(jnp.stack(lses, axis=0), axis=0)
    o = jnp.sum(w[..., None] * jnp.stack(outs, axis=0), axis=0)
    return o.astype(q.dtype)

def first_inputs(seed: int = 0) -> dict:
    key = jax.random.key(seed)
    ks = jax.random.split(key, 13)
    f32 = jnp.float32
    nrm = lambda k, shape, s: jax.random.normal(k, shape, f32) * s
    return {
        "x": jax.random.normal(ks[0], (BATCH, SEQ, D_MODEL), f32),
        "ln_pre_mix": 1.0 + nrm(ks[1], (DEPTH, D_MODEL), 0.05),
        "w_in": nrm(ks[2], (DEPTH, D_MODEL, IN_WIDTH), D_MODEL ** -0.5),
        "w_pool": nrm(ks[3], (DEPTH, len(POOL_WINDOWS), POOL_GROUP, POOL_GROUP), POOL_GROUP ** -0.5),
        "pool_scale": 1.0 + nrm(ks[4], (DEPTH, POOL_WIDTH), 0.1),
        "w_out": nrm(ks[5], (DEPTH, MIX_WIDTH, D_MODEL), MIX_WIDTH ** -0.5),
        "ln_post_mix": 1.0 + nrm(ks[6], (DEPTH, D_MODEL), 0.05),
        "ln_pre_ffn": 1.0 + nrm(ks[7], (DEPTH, D_MODEL), 0.05),
        "w_gate": nrm(ks[8], (DEPTH, D_MODEL, D_FF), D_MODEL ** -0.5),
        "w_up": nrm(ks[9], (DEPTH, D_MODEL, D_FF), D_MODEL ** -0.5),
        "w_down": nrm(ks[10], (DEPTH, D_FF, D_MODEL), D_FF ** -0.5),
        "ln_post_ffn": 1.0 + nrm(ks[11], (DEPTH, D_MODEL), 0.05),
    }

def first_block(x, ln_pre_mix, w_in, w_pool, pool_scale, w_out, ln_post_mix,
              ln_pre_ffn, w_gate, w_up, w_down, ln_post_ffn):
    B, S, _ = x.shape
    pos = jnp.arange(S)
    for l in range(DEPTH):
        h = rms_norm(x, ln_pre_mix[l])
        proj = h @ w_in[l]
        u_pool = proj[..., :POOL_WIDTH]
        q = proj[..., POOL_WIDTH:POOL_WIDTH + ATTN_WIDTH].reshape(B, S, N_HEADS, HEAD_DIM)
        k = proj[..., POOL_WIDTH + ATTN_WIDTH:POOL_WIDTH + 2 * ATTN_WIDTH].reshape(B, S, N_HEADS, HEAD_DIM)
        v = proj[..., POOL_WIDTH + 2 * ATTN_WIDTH:].reshape(B, S, N_HEADS, HEAD_DIM)
        q, k = rope(q, pos), rope(k, pos)
        pool_out = multi_scale_pool(u_pool, w_pool[l], pool_scale[l])
        attn_out = dilated_attention(q, k, v).reshape(B, S, ATTN_WIDTH)
        mix = jnp.concatenate([pool_out, attn_out], axis=-1) @ w_out[l]
        x = x + rms_norm(mix, ln_post_mix[l])
        h = rms_norm(x, ln_pre_ffn[l])
        f = (jax.nn.silu(h @ w_gate[l]) * (h @ w_up[l])) @ w_down[l]
        x = x + rms_norm(f, ln_post_ffn[l])
    return x


DEPTH_2 = 2

CHUNK = 64
N_MIXERS = 2
RET_HEADS = 4
RET_QK_DIM = 256
RET_V_DIM = 512
RET_IN = 2 * RET_HEADS * RET_QK_DIM + 2 * RET_HEADS * RET_V_DIM
SB_HEADS = 16
SB_HEAD_DIM = D_MODEL // SB_HEADS
SB_QBLOCK = 128
FFN_HIDDEN = -(-(8 * D_MODEL) // (3 * 256)) * 256
N_RET = (DEPTH_2 + 1) // 2
N_SB = DEPTH_2 // 2


def rms_norm_2(x, gain):
    xf = x.astype(jnp.float32)
    y = xf * lax.rsqrt(jnp.mean(xf * xf, axis=-1, keepdims=True) + EPS)
    return (y * gain.astype(jnp.float32)).astype(x.dtype)

def rotary(x, positions):
    d = x.shape[-1]
    inv_freq = 1.0 / (ROPE_THETA ** (jnp.arange(0, d // 2, dtype=jnp.float32) / (d // 2)))
    ang = positions.astype(jnp.float32)[:, None] * inv_freq[None, :]
    cos = jnp.cos(ang)[None, :, None, :].astype(x.dtype)
    sin = jnp.sin(ang)[None, :, None, :].astype(x.dtype)
    x1, x2 = x[..., : d // 2], x[..., d // 2:]
    return jnp.concatenate([x1 * cos - x2 * sin, x1 * sin + x2 * cos], axis=-1)

def retention(h, w_in, out_gain, w_o):
    B, S, _ = h.shape
    H, DK, DV, C = RET_HEADS, RET_QK_DIM, RET_V_DIM, CHUNK
    N = S // C
    proj = h @ w_in
    q, k, v, g = jnp.split(proj, [H * DK, 2 * H * DK, 2 * H * DK + H * DV], axis=-1)
    pos = jnp.arange(S)
    q = rotary(q.reshape(B, S, H, DK), pos)
    k = rotary(k.reshape(B, S, H, DK), pos) * (DK ** -0.5)
    v = v.reshape(B, S, H, DV)
    to_chunks = lambda t: t.reshape(B, N, C, H, t.shape[-1]).transpose(1, 0, 3, 2, 4)
    qc, kc, vc = to_chunks(q), to_chunks(k), to_chunks(v)

    log_gamma = jnp.log(1.0 - 2.0 ** (-5.0 - jnp.arange(H, dtype=jnp.float32)))
    idx = jnp.arange(C, dtype=jnp.float32)
    intra = jnp.exp(log_gamma[:, None, None] * jnp.abs(idx[:, None] - idx[None, :])).astype(q.dtype)
    q_decay = jnp.exp(log_gamma[:, None] * (idx + 1.0)).astype(q.dtype)
    k_decay = jnp.exp(log_gamma[:, None] * (C - 1.0 - idx)).astype(q.dtype)
    chunk_decay = jnp.exp(log_gamma * C).astype(q.dtype)

    scores = jnp.einsum('nbhcd,nbhed->nbhce', qc, kc) * intra
    inner = jnp.einsum('nbhce,nbhev->nbhcv', scores, vc)

    def step(state, xs):
        qn, kn, vn = xs
        cross = jnp.einsum('bhcd,bhdv->bhcv', qn * q_decay[None, :, :, None], state)
        new_state = state * chunk_decay[None, :, None, None] + jnp.einsum(
            'bhcd,bhcv->bhdv', kn * k_decay[None, :, :, None], vn)
        return new_state, cross

    state0 = jnp.zeros((B, H, DK, DV), dtype=q.dtype)
    _, cross = lax.scan(step, state0, (qc, kc, vc))
    o = (inner + cross).transpose(1, 0, 3, 2, 4).reshape(B, S, H, DV)
    o = rms_norm_2(o, out_gain)
    o = o.reshape(B, S, H * DV) * jax.nn.silu(g)
    return o @ w_o

def stick_breaking(h, w_in, q_gain, k_gain, w_o):
    B, S, _ = h.shape
    H, DH, QB = SB_HEADS, SB_HEAD_DIM, SB_QBLOCK
    q, k, v = jnp.split(h @ w_in, 3, axis=-1)
    heads = lambda t: t.reshape(B, S, H, DH).transpose(0, 2, 1, 3)
    q = rms_norm_2(heads(q), q_gain)
    k = rms_norm_2(heads(k), k_gain)
    v = heads(v)
    scale = DH ** -0.5
    outs = []
    for blk in range(S // QB):
        t0 = blk * QB
        kend = t0 + QB
        z = jnp.einsum('bhtd,bhsd->bhts', q[:, :, t0:kend], k[:, :, :kend]).astype(jnp.float32) * scale
        t_pos = t0 + jnp.arange(QB)
        s_pos = jnp.arange(kend)
        mask = s_pos[None, :] < t_pos[:, None]
        log_stay = jnp.where(mask, jax.nn.log_sigmoid(-z), 0.0)
        later = lax.cumsum(log_stay, axis=3, reverse=True) - log_stay
        weight = jnp.where(mask, jnp.exp(jax.nn.log_sigmoid(z) + later), 0.0)
        outs.append(jnp.einsum('bhts,bhsd->bhtd', weight.astype(v.dtype), v[:, :, :kend]))
    o = jnp.concatenate(outs, axis=2).transpose(0, 2, 1, 3).reshape(B, S, H * DH)
    return o @ w_o

def swiglu(h, w_in, w_out):
    gate, up = jnp.split(h @ w_in, 2, axis=-1)
    return (jax.nn.silu(gate) * up) @ w_out

def second_inputs(seed: int = 0) -> dict:
    key = jax.random.key(seed)
    ks = jax.random.split(key, 12)
    nrm = lambda k, shape, fan_in: jax.random.normal(k, shape, jnp.float32) * (fan_in ** -0.5)
    gain = lambda k, shape: 1.0 + 0.02 * jax.random.normal(k, shape, jnp.float32)
    return {
        "x": jax.random.normal(ks[0], (BATCH, SEQ, D_MODEL), jnp.float32),
        "mix_norm": gain(ks[1], (DEPTH_2, D_MODEL)),
        "ffn_norm": gain(ks[2], (DEPTH_2, D_MODEL)),
        "ret_w_in": nrm(ks[3], (N_RET, D_MODEL, RET_IN), D_MODEL),
        "ret_out_norm": gain(ks[4], (N_RET, RET_HEADS, RET_V_DIM)),
        "ret_w_o": nrm(ks[5], (N_RET, RET_HEADS * RET_V_DIM, D_MODEL), RET_HEADS * RET_V_DIM),
        "sb_w_in": nrm(ks[6], (N_SB, D_MODEL, 3 * D_MODEL), D_MODEL),
        "sb_q_norm": gain(ks[7], (N_SB, SB_HEAD_DIM)),
        "sb_k_norm": gain(ks[8], (N_SB, SB_HEAD_DIM)),
        "sb_w_o": nrm(ks[9], (N_SB, D_MODEL, D_MODEL), D_MODEL),
        "ffn_w_in": nrm(ks[10], (DEPTH_2, D_MODEL, 2 * FFN_HIDDEN), D_MODEL),
        "ffn_w_out": nrm(ks[11], (DEPTH_2, FFN_HIDDEN, D_MODEL), FFN_HIDDEN),
    }

def second_block(x, mix_norm, ffn_norm, ret_w_in, ret_out_norm, ret_w_o,
              sb_w_in, sb_q_norm, sb_k_norm, sb_w_o, ffn_w_in, ffn_w_out):
    for i in range(DEPTH_2):
        h = rms_norm_2(x, mix_norm[i])
        j = i // N_MIXERS
        if i % N_MIXERS == 0:
            x = x + retention(h, ret_w_in[j], ret_out_norm[j], ret_w_o[j])
        else:
            x = x + stick_breaking(h, sb_w_in[j], sb_q_norm[j], sb_k_norm[j], sb_w_o[j])
        x = x + swiglu(rms_norm_2(x, ffn_norm[i]), ffn_w_in[i], ffn_w_out[i])
    return x


def setup_inputs(seed=0):
    out = dict(first_inputs(seed))
    for name, value in second_inputs(seed + 1).items():
        if name != "x":
            out[name + "_2"] = value
    return out


def reference(
    x, ln_pre_mix, w_in, w_pool, pool_scale, w_out, ln_post_mix, ln_pre_ffn, w_gate, w_up,
    w_down, ln_post_ffn, mix_norm_2, ffn_norm_2, ret_w_in_2, ret_out_norm_2, ret_w_o_2,
    sb_w_in_2, sb_q_norm_2, sb_k_norm_2, sb_w_o_2, ffn_w_in_2, ffn_w_out_2,
):
    x = first_block(
        x, ln_pre_mix, w_in, w_pool, pool_scale, w_out, ln_post_mix, ln_pre_ffn, w_gate, w_up,
        w_down, ln_post_ffn,
    )
    return second_block(
        x, mix_norm_2, ffn_norm_2, ret_w_in_2, ret_out_norm_2, ret_w_o_2, sb_w_in_2,
        sb_q_norm_2, sb_k_norm_2, sb_w_o_2, ffn_w_in_2, ffn_w_out_2,
    )


_drawn_inputs = setup_inputs


def setup_inputs(seed=0):
    import zlib

    import numpy as np

    out = dict(_drawn_inputs(seed))
    spreads = {}
    factors = {'mix_norm_2': 3.348,
     'ffn_norm_2': 4.622,
     'ret_out_norm_2': 7.667,
     'sb_q_norm_2': 99.496,
     'sb_k_norm_2': 99.315}
    for name, (base, spread) in spreads.items():
        noise = np.random.default_rng([zlib.crc32(name.encode()), seed]).standard_normal(out[name].shape)
        drawn = base * np.exp(spread * noise) if base else spread * noise
        out[name] = __import__('jax').numpy.asarray(drawn.astype(out[name].dtype))
    for name, factor in factors.items():
        out[name] = (out[name] * factor).astype(out[name].dtype)
    return out
```

```python
from contextlib import ExitStack

import numpy as np

import concourse.bass as bass
from concourse import mybir

P = 128
T = 512
D = 1024
DC = D // P
FF = 2816
FC = FF // P
HALF = FC // 2
POOL_TILES = 2
PAIRS1 = 6
RET_H, RET_QT, RET_VT = 4, 2, 4
PAIRS3 = 8
TB = T // P
EPS = 1e-6

ALU = mybir.AluOpType
ACT = mybir.ActivationFunctionType
F32 = mybir.dt.float32
F32R = mybir.dt.float32r

U_POOL = 0
U_ATTN = U_POOL + POOL_TILES
U_OUT1 = U_ATTN + 3 * PAIRS1
U_FFN1 = U_OUT1 + DC
U_DOWN1 = U_FFN1 + 2 * FC
U_RET = U_DOWN1 + 2 * DC
RET_UNITS = 2 * RET_QT + 2 * RET_VT
U_RETO = U_RET + RET_H * RET_UNITS
U_FFN2 = U_RETO + 2 * DC
U_DOWN2 = U_FFN2 + 2 * FC
U_SB = U_DOWN2 + 2 * DC
U_OUT3 = U_SB + 3 * PAIRS3
U_FFN3 = U_OUT3 + DC
U_DOWN3 = U_FFN3 + 2 * FC
U_END = U_DOWN3 + 2 * DC
STRETCHES = [(U_DOWN1, DC, False), (2 * DC, HALF, True), (U_DOWN2 - U_RET, DC, False), (2 * DC, HALF, True),
             (U_DOWN3 - U_SB, DC, False), (2 * DC, HALF, True)]

G_MIX1, G_POST1, G_FFN1, G_POSTF1, G_MIX2, G_FFN2, G_MIX3, G_FFN3 = (DC * n for n in range(8))
G_POOL = 8 * DC
G_RET = G_POOL + POOL_TILES
G_Q = G_RET + RET_H * RET_VT
G_K = G_Q + 1
G_EPS = G_K + 1
G_COLS = G_EPS + 1

WIDE = 1280
T_AT = [0, 512, 1024, 896]
S_AT = [896, 1024, 512, 0]


def t_width(block):
    return T - P * block


def s_width(block):
    return P * (block + 1)


def chunks_of(unit):
    if unit >= U_END:
        return 0
    at = 0
    for count, chunks, _ in STRETCHES:
        at += count
        if unit < at:
            return chunks


class Unit:

    def __init__(self, first, i=0, step=0):
        assert step % 2 == 0
        self.s = first % 2
        self.m = i * (step // 2) + first // 2 if step else first // 2
        self.first = first

    def __add__(self, n):
        u = Unit(self.first + n)
        u.m = self.m + ((self.first + n) // 2 - self.first // 2)
        return u

    @property
    def index(self):
        return self.m * 2 + self.s


class Steps:

    def __init__(self, eng, sem):
        self.eng, self.sem, self.base, self.n, self.start = eng, sem, 0, 0, 0

    def at(self, index, per):
        self.n = 0
        self.base = index * per + self.start

    def end(self, count=None):
        self.start += self.n if count is None else count
        self.base, self.n = self.start, 0

    def done(self, ins):
        ins.then_inc(self.sem, 1)
        self.n += 1

    def wait(self, back=0):
        self.eng.wait_ge(self.sem, self.base + self.n - back)


def build(nc, ins, out_t):
    ctx = ExitStack()
    with ctx:
        def alloc(stack, name, shape, dt=F32):
            return stack.enter_context(nc.sbuf_tensor(name, shape, dt))

        def sb(name, shape, dt=F32):
            return alloc(ctx, name, shape, dt)

        def sem(name):
            return ctx.enter_context(nc.semaphore(name))

        X = sb("X", [P, DC, T])
        HH = sb("HH", [P, DC, T], F32R)
        HL = sb("HL", [P, DC, T], F32R)
        RAW = [sb(f"RAW{s}", [P, HALF, P]) for s in range(2)]
        WH = [sb(f"WH{s}", [P, HALF, P], F32R) for s in range(2)]
        WL = [sb(f"WL{s}", [P, HALF, P], F32R) for s in range(2)]
        RB = sb("RB", [P, T])
        ACC = sb("ACC", [P, T])
        SQ = [sb(f"SQ{s}", [P, T]) for s in range(2)]
        GAINS = sb("GAINS", [P, G_COLS])
        IDENT = sb("IDENT", [P, P])
        MEAN = sb("MEAN", [P, P])

        def scratch(tensors):
            with ExitStack() as stack:
                return [alloc(stack, *t) for t in tensors]

        MH, ML, G1, SG, U1, HD, F = scratch([
            ("MH", [P, FC, T], F32R), ("ML", [P, FC, T], F32R), ("G1", [P, T]), ("SG", [P, T]),
            ("U1", [P, T]), ("HD", [P, T]), ("F", [P, DC, T])])
        pad = 16
        (M1H, M1L, QT1, KT1, VZ1, QC, RT, PR, PT, BIAS, CS1, SN1, SWAP, V1, MX, NM, DEN, RD,
         UP, WA, WB, INV, DF, YT, WPOOL) = scratch([
             ("M1H", [P, DC, T], F32R), ("M1L", [P, DC, T], F32R), ("QT1", [P, 2, T]), ("KT1", [P, 2, T]),
             ("VZ1", [P, 2, 2, TB, P]), ("QC", [P, 2, T]), ("RT", [P, 2, T]), ("PR", [P, 2, WIDE]),
             ("PT", [P, 2, WIDE]), ("BIAS", [P, T]), ("CS1", [P, T]), ("SN1", [P, T]), ("SWAP", [P, P]),
             ("V1", [P, T]), ("MX", [P, 2, TB]), ("NM", [P, 2, TB]), ("DEN", [P, 2, TB]), ("RD", [P, 2, TB]),
             ("UP", [P, POOL_TILES, pad + T]), ("WA", [P, pad + T]), ("WB", [P, pad + T]),
             ("INV", [P, POOL_TILES, T]), ("DF", [P, POOL_TILES, T]), ("YT", [P, T]), ("WPOOL", [P, POOL_TILES, P])])
        M2H, M2L, CS2, SN2, DECAY, QT2, KT2, SC2, VT2, O2, SG2, TA, TC = scratch([
            ("M2H", [P, RET_H * RET_VT, T], F32R), ("M2L", [P, RET_H * RET_VT, T], F32R), ("CS2", [P, T]),
            ("SN2", [P, T]), ("DECAY", [P, T]), ("QT2", [P, RET_QT, T]), ("KT2", [P, RET_QT, T]), ("SC2", [P, WIDE]),
            ("VT2", [P, TB, T]), ("O2", [P, RET_VT, T]), ("SG2", [P, RET_VT, T]), ("TA", [P, T]), ("TC", [P, T])])
        (M3H, M3L, QT3, KT3, VZ3, QS, V3, RQ, ZS, LG, SP, SPH, SPL, MASK, TRI32, LATER, ALL, HEADMEAN) = scratch([
            ("M3H", [P, DC, T], F32R), ("M3L", [P, DC, T], F32R), ("QT3", [P, 2, T]), ("KT3", [P, 2, T]),
            ("VZ3", [P, 2, 2, TB, P]), ("QS", [P, 2, T]), ("V3", [P, T]), ("RQ", [P, 2, T]), ("ZS", [P, 2, WIDE]),
            ("LG", [P, 2, WIDE]), ("SP", [P, 2, WIDE]), ("SPH", [P, 2, WIDE], F32R), ("SPL", [P, 2, WIDE], F32R),
            ("MASK", [P, T]), ("TRI32", [P, 2 * P]), ("LATER", [P, P], F32R), ("ALL", [P, P], F32R),
            ("HEADMEAN", [P, P])])

        CONSTS = [(IDENT[:], "ident"), (MEAN[:], "mean"), (BIAS[:], "bias"), (CS1[:], "cos1"), (SN1[:], "sin1"),
                  (SWAP[:], "swap"), (INV[:], "inv_counts"), (WPOOL[:], "w_pool")]
        N_CONST = len(CONSTS)
        SUMS = {0: 1, 1: 2, 3: 3, 5: 4, 6: 5, 7: 6}

        B = [ctx.enter_context(nc.psum_tensor(f"B{n}", [P, T], F32)) for n in range(8)]

        s_raw = [sem(f"raw_landed{s}") for s in range(2)]
        s_hi = sem("weights_hi")
        s_lo = sem("weights_lo")
        s_hi_used = sem("weights_hi_used")
        s_unit = sem("unit_done")
        s_x_in = sem("x_landed")
        s_const = sem("constants_landed")
        s_squared = sem("squared")
        s_sq_used = sem("square_added")
        s_zeroed = sem("sum_zeroed")
        s_mean = sem("mean_ready")
        s_root = sem("root_ready")
        s_rb = sem("rnorm_ready")
        s_h_hi = sem("input_hi")
        s_h = sem("input_ready")
        s_taken = sem("tile_taken")
        s_x_new = sem("x_updated")
        s_out = sem("output_stored")
        s_gate = sem("gate_scaled")
        s_silu = sem("silu_done")
        s_up = sem("up_scaled")
        s_hidden = sem("hidden_done")
        s_m_hi = sem("mixed_hi")
        s_m = sem("mixed_ready")
        s_dve = sem("vector_steps")
        s_act = sem("scalar_steps")

        def gain(base, c):
            return GAINS[:, bass.ds(c + base, 1)]

        def wait_unit(eng, u):
            eng.wait_ge(s_unit, u.index + 1)

        def split_hi(act, u, chunks):
            if not chunks:
                return
            act.wait_ge(s_raw[u.s], u.m * 16 + 16)
            if not (isinstance(u.m, int) and u.index < 2):
                act.wait_ge(s_hi_used, u.index - 1)
            act.copy(WH[u.s][:, 0:chunks, :], RAW[u.s][:, 0:chunks, :]).then_inc(s_hi, 1)

        def use_unit(pe, u, bank, chunks, xh, xl, k0=0, start=True, stop=True, before=None):
            wh, wl = WH[u.s], WL[u.s]
            pe.wait_ge(s_hi, u.index + 1)
            for c in range(chunks):
                if before is not None:
                    before(k0 + c)
                pe.matmul(bank, wh[:, c, :], xh[:, k0 + c, :], start=(start and c == 0), stop=False)
                mm = pe.matmul(bank, wh[:, c, :], xl[:, k0 + c, :], start=False, stop=False)
            mm.then_inc(s_hi_used, 1)
            pe.wait_ge(s_lo, u.index + 1)
            for c in range(chunks):
                mm = pe.matmul(bank, wl[:, c, :], xh[:, k0 + c, :], start=False,
                               stop=(stop and c == chunks - 1))
            mm.then_inc(s_unit, 1)

        block = ctx.enter_context(nc.Block())

        M_BASE = [0, PAIRS1, PAIRS1 + FC, PAIRS1 + FC + 16, PAIRS1 + 2 * FC + 16, PAIRS1 + 2 * FC + 16 + PAIRS3]

        a_copied = sem("a_qk_copied")
        a_swapped = sem("a_qk_swapped")
        a_qk = sem("a_qk_ready")
        a_vs = sem("a_v_scaled")
        a_vt = sem("a_v_turned")
        a_v = sem("a_v_ready")
        a_scores = sem("a_scores_ready")
        a_mask_start = sem("a_masking_started")
        a_masked = sem("a_scores_masked")
        a_negmax = sem("a_negmax_ready")
        a_exp = sem("a_exp_done")
        a_probs = sem("a_probs_ready")
        a_turned = sem("a_probs_turned")
        a_pt_act = sem("a_probs_copied_scalar")
        a_pt_dve = sem("a_probs_copied_vector")
        a_pv = sem("a_values_summed")
        a_zero = sem("a_zeroed")
        p_u = sem("p_u_ready")
        p_d = sem("p_differences_ready")
        p_y = sem("p_products_ready")
        p_yt = sem("p_scaled")
        p_hi = sem("p_hi")
        p_m = sem("p_ready")
        r_tab = sem("r_tables_landed")
        r_dec = sem("r_decay_landed")
        r_cs = sem("r_tables_scaled")
        r_qk = sem("r_qk_ready")
        r_taken = sem("r_bank_taken")
        r_sc = sem("r_scores_ready")
        r_w = sem("r_scores_weighted")
        r_vt = sem("r_v_turned")
        r_v = sem("r_v_ready")
        r_g = sem("r_gate_scaled")
        r_sg = sem("r_gate_silu")
        r_pv = sem("r_values_summed")
        r_oc = sem("r_values_copied")
        r_sq = sem("r_squared")
        r_acc = sem("r_squares_added")
        r_mean = sem("r_mean_ready")
        r_root = sem("r_root_ready")
        r_ro = sem("r_rnorm_ready")
        r_p = sem("r_products_ready")
        b_tab = sem("b_tables_landed")
        b_tri = sem("b_tables_copied")
        b_qs = sem("b_qk_scaled")
        b_sq = sem("b_qk_squared")
        b_mean = sem("b_qk_mean")
        b_rq = sem("b_qk_rnorm")
        b_qk = sem("b_qk_ready")
        b_vs = sem("b_v_scaled")
        b_vt = sem("b_v_turned")
        b_v = sem("b_v_ready")
        b_z = sem("b_z_ready")
        b_zs = sem("b_z_copied")
        b_na = sem("b_negabs_ready")
        b_lg = sem("b_log_ready")
        b_sp = sem("b_softplus_ready")
        b_hi = sem("b_softplus_hi")
        b_lo = sem("b_softplus_lo")
        b_later = sem("b_later_ready")
        b_arg = sem("b_exponent_ready")
        b_w = sem("b_weights_ready")
        b_pv = sem("b_values_summed")
        b_zero = sem("b_zeroed")

        TAKEN = 8

        @block.sync
        def _(sp):
            def load_unit(u, source, chunks):
                if not (isinstance(u.m, int) and u.index < 2):
                    sp.wait_ge(s_lo, u.index - 1)
                sp.dma_start(RAW[u.s][:, 0:chunks, :], source).then_inc(s_raw[u.s], 16)

            at = {False: 0, True: 0}
            first = 0
            for count, chunks, large in STRETCHES:
                stream = ins["w_large" if large else "w_small"].rearrange("u p (c n) -> u p c n", c=chunks)
                start = 0
                if first == 0:
                    for n in range(2):
                        load_unit(Unit(n), stream[n], chunks)
                    start = 1
                with sp.Fori(start, count // 2) as i:
                    for n in range(2):
                        load_unit(Unit(first + n, i, 2), stream[i * 2 + (at[large] + n)], chunks)
                first += count
                at[large] += count
            for c in range(DC):
                sp.wait_ge(s_taken, 8 * 5 + c + 1)
                sp.dma_start(out_t[:, c, :], X[:, c, :]).then_inc(s_out, 16)
            sp.wait_ge(s_out, 16 * DC)

        @block.gpsimd
        def _(pool):
            def split_lo(u, chunks):
                pool.wait_ge(s_hi, u.index + 1)
                if not (isinstance(u.m, int) and u.index < 2):
                    pool.wait_ge(s_unit, u.index - 1)
                pool.tensor_tensor(WL[u.s][:, 0:chunks, :], RAW[u.s][:, 0:chunks, :],
                                   WH[u.s][:, 0:chunks, :].bitcast(F32), ALU.subtract).then_inc(s_lo, 1)

            pool.memset(VZ1[:], 0.0).then_inc(a_zero, 1)
            pool.memset(UP[:], 0.0).then_inc(a_zero, 1)
            pool.memset(WA[:], 0.0).then_inc(a_zero, 1)
            pool.memset(WB[:], 0.0).then_inc(a_zero, 1)
            first = 0
            for count, chunks, _ in STRETCHES:
                start = 0
                if first == 0:
                    for n in range(2):
                        split_lo(Unit(n), chunks)
                    start = 1
                if first == U_SB:
                    pool.wait_ge(s_unit, U_SB)
                    pool.memset(VZ3[:], 0.0).then_inc(b_zero, 1)
                with pool.Fori(start, count // 2) as i:
                    for n in range(2):
                        split_lo(Unit(first + n, i, 2), chunks)
                first += count

        @block.tensor
        def _(pe):
            def mean_of_sum(n):
                pe.wait_ge(s_sq_used, 8 * n + 8)
                pe.matmul(B[7][:], MEAN[:], ACC[:], start=True, stop=True).then_inc(s_mean, 1)

            def ready_h(which):
                return lambda k: pe.wait_ge(s_h, 8 * which + k + 1)

            def ready_h_and_mean(which, n):
                def before(k):
                    pe.wait_ge(s_squared, 8 * n + k + 1)
                    pe.matmul(B[7][:], MEAN[:], SQ[k % 2][:], start=(k == 0), stop=(k == DC - 1),
                              skip_group_check=True).then_inc(s_sq_used, 1)
                    pe.wait_ge(s_h, 8 * which + k + 1)
                return before

            def ffn(f, u0, before, n=None):
                def pair(i, before=None):
                    if before is None:
                        pe.wait_ge(s_gate, i + FC * f)
                        pe.wait_ge(s_up, i + FC * f)
                    use_unit(pe, Unit(u0, i, 2), B[0][:], DC, HH, HL, before=before)
                    if before is not None and n is not None:
                        mean_of_sum(n)
                    use_unit(pe, Unit(u0 + 1, i, 2), B[1][:], DC, HH, HL)
                pair(0, before)
                with pe.Fori(1, FC) as i:
                    pair(i)

            def outputs(o, u0, per, chunks, xh, xl, before):
                def two(i, before=None):
                    for b in range(2):
                        if before is None:
                            pe.wait_ge(s_taken, i * 2 + (8 * o + b - 1))
                        for q in range(per):
                            use_unit(pe, Unit(u0 + per * b + q, i, 2 * per), B[b][:], chunks, xh, xl,
                                     k0=chunks * q, start=(q == 0), stop=(q == per - 1),
                                     before=before if b == 0 else None)
                two(0, before)
                with pe.Fori(1, DC // 2) as i:
                    two(i)

            def attn_stage(j, jp, a, ap):
                u = None if j is None else Unit(U_ATTN + 3 * jp, j[1], 6)
                jj = None if j is None else j[0]

                def scores(h):
                    hd = a * 2 + h
                    pe.wait_ge(a_qk, a * 2 + 2)
                    if not (isinstance(a, int) and a * 2 + h == 0):
                        pe.wait_ge(a_masked, hd * 4)
                        pe.wait_ge(a_pt_dve, hd * 2)
                    r = slice(64 * h, 64 * h + 64)
                    for tb, (bank, at) in ((3, (2, 0)), (2, (3, 0)), (0, (3, 384)), (1, (4, 0))):
                        w = s_width(tb)
                        mm = pe.matmul(B[bank][:, at:at + w], QT1[r, ap, P * tb:P * tb + P], KT1[r, ap, 0:w],
                                       start=True, stop=True)
                    mm.then_inc(a_scores, 1)

                def turn(h):
                    hd = a * 2 + h
                    pe.wait_ge(a_probs, hd * 4 + 4)
                    if not (isinstance(a, int) and a * 2 + h == 0):
                        pe.wait_ge(a_pt_act, hd)
                        pe.wait_ge(a_pt_dve, hd * 2)
                    for blocks in (((0, 5, 0),), ((1, 6, 0), (3, 6, 384)), ((2, 4, 256),)):
                        for sb_, bank, at in blocks:
                            for tb in range(sb_, TB):
                                col = S_AT[tb] + P * sb_
                                o = at + P * (tb - sb_)
                                mm = pe.transpose(B[bank][:, o:o + P], PR[:, h, col:col + P], IDENT[:])
                        mm.then_inc(a_turned, 1)

                def values(h):
                    hd = a * 2 + h
                    pe.wait_ge(a_pt_act, hd + 1)
                    pe.wait_ge(a_pt_dve, hd * 2 + 2)
                    if h == 0:
                        pe.wait_ge(a_v, a * 2 + 2)
                        if not (isinstance(a, int) and a == 0):
                            pe.wait_ge(s_m, a)
                    for sb_ in range(TB):
                        w = t_width(sb_)
                        mm = pe.matmul(B[7][:, P * sb_:T], VZ1[:, ap, h, sb_, :],
                                       PT[:, h, T_AT[sb_]:T_AT[sb_] + w], start=(h == 0 and sb_ == 0),
                                       stop=(h == 1 and sb_ == TB - 1), skip_group_check=True)
                    mm.then_inc(a_pv, 1)

                def swap(n):
                    pe.wait_ge(a_copied, jj * 2 + n + 1)
                    pe.matmul(B[n][:], SWAP[:], QC[:, n, :], start=True, stop=True).then_inc(a_swapped, 1)

                first = isinstance(jj, int) and jj == 0
                if a is not None:
                    scores(0)
                if j is not None:
                    if not first:
                        pe.wait_ge(a_v, jj * 2)
                    else:
                        pe.wait_ge(p_u, 1)
                    use_unit(pe, u, B[0][:], DC, HH, HL)
                if a is not None:
                    turn(0)
                if j is not None:
                    if not first:
                        pe.wait_ge(a_qk, jj * 2)
                    else:
                        pe.wait_ge(p_u, 2)
                    use_unit(pe, u + 1, B[1][:], DC, HH, HL)
                    swap(0)
                if a is not None:
                    values(0)
                    scores(1)
                if j is not None:
                    pe.wait_ge(a_qk, jj * 2 + 1)
                    use_unit(pe, u + 2, B[0][:], DC, HH, HL)
                    swap(1)
                if a is not None:
                    turn(1)
                if j is not None:
                    pe.wait_ge(a_vs, jj + 1)
                    for tb in range(TB):
                        mm = pe.transpose(B[0][:, P * tb:P * tb + P], V1[:, P * tb:P * tb + P], IDENT[:])
                    mm.then_inc(a_vt, 1)
                if a is not None:
                    values(1)

            pe.wait_ge(s_const, 16 * N_CONST)
            use_unit(pe, Unit(0), B[0][:], DC, HH, HL, before=ready_h(0))
            mean_of_sum(0)
            use_unit(pe, Unit(1), B[1][:], DC, HH, HL)
            attn_stage((0, 0), 0, None, None)
            for t in range(POOL_TILES):
                pe.wait_ge(p_d, t + 1)
                pe.matmul(B[5 + t][:], WPOOL[:, t, :], DF[:, t, :], start=True, stop=True).then_inc(p_y, 1)
            pe.wait_ge(p_m, 2)
            attn_stage((1, 0), 1, 0, 0)
            with pe.Fori(0, PAIRS1 // 2 - 1) as i:
                attn_stage((i * 2 + 2, i + 1), 0, i * 2 + 1, 1)
                attn_stage((i * 2 + 3, i + 1), 1, i * 2 + 2, 0)
            attn_stage(None, None, PAIRS1 - 1, 1)

            pe.wait_ge(a_v, 2 * PAIRS1)
            pe.wait_ge(a_qk, 2 * PAIRS1)

            def ready_m1(k):
                if k >= POOL_TILES:
                    pe.wait_ge(s_m, k - POOL_TILES + 1)
            outputs(0, U_OUT1, 1, DC, M1H, M1L, ready_m1)
            mean_of_sum(1)
            ffn(0, U_FFN1, ready_h_and_mean(1, 2))
            pe.wait_ge(s_gate, FC)
            pe.wait_ge(s_up, FC)
            outputs(1, U_DOWN1, 2, HALF, MH, ML, lambda k: pe.wait_ge(s_m, M_BASE[1] + k + 1))
            mean_of_sum(3)

            def ret_head(h, first):
                def unit(n):
                    return Unit(U_RET + n, h, RET_UNITS)

                def project(n, bank, before=None):
                    use_unit(pe, unit(n), B[bank][:], DC, HH, HL, before=before)

                def turn_v(d, bank):
                    pe.wait_ge(r_taken, h * TAKEN + (4 + d + 1))
                    for tb in range(TB):
                        mm = pe.transpose(B[bank][:, P * tb:P * tb + P], (TA if d % 2 == 0 else TC)[:, P * tb:P * tb + P],
                                          IDENT[:])
                    mm.then_inc(r_vt, 1)

                def values(d, bank):
                    pe.wait_ge(r_v, h * RET_VT + (d + 1))
                    if d == 0:
                        pe.wait_ge(r_w, h * TB + 4)
                    if d == 3:
                        pe.wait_ge(r_sq, h * RET_VT + 1)
                    for sb_ in range(TB):
                        mm = pe.matmul(B[bank][:, P * sb_:T], VT2[:, sb_, P * d:P * d + P],
                                       SC2[:, T_AT[sb_]:T_AT[sb_] + t_width(sb_)], start=(sb_ == 0),
                                       stop=(sb_ == TB - 1))
                    mm.then_inc(r_pv, 1)

                if first:
                    project(0, 0, before=ready_h_and_mean(2, 4))
                else:
                    pe.wait_ge(r_g, h * RET_VT)
                    project(0, 0)
                project(1, 1)
                project(2, 2)
                project(3, 3)
                pe.wait_ge(r_taken, h * TAKEN + 2)
                project(4, 0)
                pe.wait_ge(r_qk, h * 4 + 4)
                if not first:
                    pe.wait_ge(r_sq, h * RET_VT)
                for sb_, bank, at in ((0, 4, 0), (1, 5, 0), (3, 5, 384), (2, 6, 0)):
                    w = t_width(sb_)
                    for c in range(RET_QT):
                        mm = pe.matmul(B[bank][:, at:at + w], KT2[:, c, P * sb_:P * sb_ + P], QT2[:, c, P * sb_:T],
                                       start=(c == 0), stop=(c == RET_QT - 1))
                    mm.then_inc(r_sc, 1)
                project(5, 1)
                turn_v(0, 0)
                pe.wait_ge(r_taken, h * TAKEN + 4)
                project(6, 2)
                turn_v(1, 1)
                project(7, 3)
                turn_v(2, 2)
                pe.wait_ge(r_v, h * RET_VT + 1)
                project(8, 0)
                turn_v(3, 3)
                values(0, 4)
                pe.wait_ge(r_v, h * RET_VT + 2)
                project(9, 1)
                values(1, 5)
                pe.wait_ge(r_v, h * RET_VT + 3)
                project(10, 2)
                values(2, 6)
                values(3, 4)
                pe.wait_ge(r_v, h * RET_VT + 4)
                project(11, 3)
                pe.wait_ge(r_acc, h * 3 + 3)
                pe.matmul(B[7][:], MEAN[:], ACC[:], start=True, stop=True).then_inc(r_mean, 1)

            pe.wait_ge(s_taken, 8 * 2)
            ret_head(0, True)
            with pe.Fori(1, RET_H) as h:
                ret_head(h, False)

            pe.wait_ge(r_g, RET_H * RET_VT)
            outputs(2, U_RETO, 2, DC, M2H, M2L, lambda k: pe.wait_ge(s_m, M_BASE[2] + k + 1))
            pe.wait_ge(s_taken, 8 * 3)
            ffn(1, U_FFN2, ready_h(3), n=5)
            pe.wait_ge(s_gate, 2 * FC)
            pe.wait_ge(s_up, 2 * FC)
            outputs(3, U_DOWN2, 2, HALF, MH, ML, lambda k: pe.wait_ge(s_m, M_BASE[3] + k + 1))

            def stick_stage(j, jp, a, ap, first_input=None):
                u = None if j is None else Unit(U_SB + 3 * jp, j[1], 6)
                jj = None if j is None else j[0]
                first = isinstance(jj, int) and jj == 0

                def z(h):
                    hd = a * 2 + h
                    pe.wait_ge(b_qk, a * 2 + 2)
                    if not (isinstance(a, int) and a * 2 + h == 0):
                        pe.wait_ge(b_zs, hd * 4)
                        if h == 0:
                            pe.wait_ge(b_arg, hd * 3)
                    r = slice(64 * h, 64 * h + 64)
                    for sb_, bank, at in ((0, 2, 0), (1, 3, 0), (3, 3, 384), (2, 4, 0)):
                        w = t_width(sb_)
                        mm = pe.matmul(B[bank][:, at:at + w], KT3[r, ap, P * sb_:P * sb_ + P],
                                       QT3[r, ap, P * sb_:T], start=True, stop=True)
                        mm.then_inc(b_z, 1)

                def later(h):
                    hd = a * 2 + h
                    pe.wait_ge(b_lo, hd + 1)
                    if h == 0:
                        pe.wait_ge(b_zs, hd * 4 + 8)
                    else:
                        pe.wait_ge(b_arg, hd * 3)
                    for sb_, bank, at in ((0, 2, 0), (1, 3, 0), (3, 3, 384), (2, 4, 0)):
                        w = t_width(sb_)
                        for n, part in enumerate((SPH, SPL)):
                            mm = pe.matmul(B[bank][:, at:at + w], LATER[:], part[:, h, T_AT[sb_]:T_AT[sb_] + w],
                                           start=(n == 0 and sb_ != 3), stop=(n == 1 and sb_ == TB - 1),
                                           skip_group_check=True)
                        for s2 in range(sb_ + 1, TB):
                            w2 = t_width(s2)
                            o = at + P * (s2 - sb_)
                            for n, part in enumerate((SPH, SPL)):
                                mm = pe.matmul(B[bank][:, o:o + w2], ALL[:], part[:, h, T_AT[s2]:T_AT[s2] + w2],
                                               start=False, stop=(n == 1 and s2 == TB - 1 and sb_ != 1),
                                               skip_group_check=True)
                        if sb_ != 1:
                            mm.then_inc(b_later, 1)

                def values(h):
                    hd = a * 2 + h
                    pe.wait_ge(b_w, hd + 1)
                    if h == 0:
                        pe.wait_ge(b_v, a * 2 + 2)
                        if not (isinstance(a, int) and a == 0):
                            pe.wait_ge(s_m, a + M_BASE[4])
                    for sb_ in range(TB):
                        w = t_width(sb_)
                        mm = pe.matmul(B[7][:, P * sb_:T], VZ3[:, ap, h, sb_, :],
                                       ZS[:, h, T_AT[sb_]:T_AT[sb_] + w], start=(h == 0 and sb_ == 0),
                                       stop=(h == 1 and sb_ == TB - 1), skip_group_check=True)
                    mm.then_inc(b_pv, 1)

                def head_mean(n):
                    pe.wait_ge(b_sq, jj * 2 + n + 1)
                    if not first:
                        pe.wait_ge(b_rq, jj * 2 + n - 1)
                    pe.matmul(B[5 + n][:], HEADMEAN[:], SQ[n][:], start=True, stop=True).then_inc(b_mean, 1)

                if a is not None:
                    z(0)
                if j is not None:
                    if not first:
                        pe.wait_ge(b_vs, jj)
                        use_unit(pe, u, B[0][:], DC, HH, HL)
                    else:
                        pe.wait_ge(s_taken, 8 * 4)
                        use_unit(pe, u, B[0][:], DC, HH, HL, before=ready_h(4))
                        mean_of_sum(6)
                if a is not None:
                    z(1)
                if j is not None:
                    if not first:
                        pe.wait_ge(b_v, jj * 2)
                    use_unit(pe, u + 1, B[1][:], DC, HH, HL)
                    head_mean(0)
                if a is not None:
                    later(0)
                if j is not None:
                    pe.wait_ge(b_qs, jj * 2 + 1)
                    use_unit(pe, u + 2, B[0][:], DC, HH, HL)
                    head_mean(1)
                if a is not None:
                    later(1)
                    values(0)
                if j is not None:
                    pe.wait_ge(b_vs, jj + 1)
                    pe.wait_ge(b_qs, jj * 2 + 2)
                    for tb in range(TB):
                        mm = pe.transpose(B[1][:, P * tb:P * tb + P], V3[:, P * tb:P * tb + P], IDENT[:])
                    mm.then_inc(b_vt, 1)
                if a is not None:
                    values(1)

            pe.wait_ge(b_tri, 2)
            stick_stage((0, 0), 0, None, None)
            stick_stage((1, 0), 1, 0, 0)
            with pe.Fori(0, PAIRS3 // 2 - 1) as i:
                stick_stage((i * 2 + 2, i + 1), 0, i * 2 + 1, 1)
                stick_stage((i * 2 + 3, i + 1), 1, i * 2 + 2, 0)
            stick_stage(None, None, PAIRS3 - 1, 1)

            pe.wait_ge(b_v, 2 * PAIRS3)
            outputs(4, U_OUT3, 1, DC, M3H, M3L, lambda k: pe.wait_ge(s_m, M_BASE[4] + k + 1))
            pe.wait_ge(s_taken, 8 * 5)
            ffn(2, U_FFN3, ready_h(5), n=7)
            pe.wait_ge(s_gate, 3 * FC)
            pe.wait_ge(s_up, 3 * FC)
            outputs(5, U_DOWN3, 2, HALF, MH, ML, lambda k: pe.wait_ge(s_m, M_BASE[5] + k + 1))

        @block.scalar
        def _(act):
            EPSC = GAINS[:, G_EPS:G_EPS + 1]

            def square(n, c, b, src):
                if not (n == 0 and isinstance(c, int) and c < 2):
                    act.wait_ge(s_sq_used, c + (8 * n - 1))
                act.activation(SQ[b][:], src, ACT.Square).then_inc(s_squared, 1)

            def input_hi(c, g):
                act.activation(HH[:, c, :], X[:, c, :], ACT.Copy, scale=gain(g, c)).then_inc(s_h_hi, 1)

            def root(n, direct=False):
                if direct:
                    act.wait_ge(s_sq_used, 8 * n + 8)
                else:
                    act.wait_ge(s_mean, SUMS[n])
                act.activation(ACC[:], B[7][:], ACT.Sqrt, bias=EPSC).then_inc(s_root, 1)

            def ffn(f, u0, chunks_after):
                def pair(i, chunks):
                    split_hi(act, Unit(u0 + 2, i, 2), chunks)
                    act.wait_ge(s_gate, i + (FC * f + 1))
                    act.activation(SG[:], G1[:], ACT.Silu).then_inc(s_silu, 1)
                    split_hi(act, Unit(u0 + 3, i, 2), chunks)
                    act.wait_ge(s_hidden, i + (FC * f + 1))
                    act.copy(MH[:, i, :], HD[:]).then_inc(s_m_hi, 1)
                with act.Fori(0, FC - 1) as i:
                    pair(i, DC)
                pair(FC - 1, chunks_after)

            def outputs(o, n, u0, per, chunks, chunks_after, gain_post=None, gain_next=None):
                def two(i, after):
                    for b in range(2):
                        c = i * 2 + b
                        for q in range(per):
                            split_hi(act, Unit(u0 + per * b + q + 2, i, 2 * per),
                                     after if per * b + q + 2 >= 2 * per else chunks)
                        if gain_post is not None:
                            act.wait_ge(s_unit, Unit(u0 + per * b + per - 1, i, 2 * per).index + 1)
                            square(n, c, b, B[b][:])
                            act.activation(F[:, c, :], B[b][:], ACT.Copy, scale=gain(gain_post, c))\
                               .then_inc(s_taken, 1)
                        elif gain_next is not None:
                            act.wait_ge(s_taken, c + (8 * o + 1))
                            square(n, c, b, X[:, c, :])
                            input_hi(c, gain_next)
                with act.Fori(0, DC // 2 - 1) as i:
                    two(i, chunks)
                two(DC // 2 - 1, chunks_after)

            def after_post(n, g, updated):
                for c in range(DC):
                    act.wait_ge(s_x_new, updated + c + 1)
                    square(n, c, c % 2, X[:, c, :])
                    input_hi(c, g)

            act.dma_start(GAINS[:], ins["gains"]).then_inc(s_x_in, 16)
            for c in range(DC):
                act.dma_start(X[:, c, :], ins["x_t"][:, c, :]).then_inc(s_x_in, 16)
            for dst, name in CONSTS:
                act.dma_start(dst, ins[name]).then_inc(s_const, 16)
            act.wait_ge(s_x_in, 16 * (DC + 1))
            for c in range(DC):
                square(0, c, c % 2, X[:, c, :])
                input_hi(c, G_MIX1)
                if c == 0:
                    split_hi(act, Unit(0), DC)
            split_hi(act, Unit(1), DC)
            root(0)
            split_hi(act, Unit(2), DC)
            split_hi(act, Unit(3), DC)

            def attn_stage(j, jp, a, ap):
                u = None if j is None else Unit(U_ATTN + 3 * jp, j[1], 6)
                jj = None if j is None else j[0]
                first = isinstance(jj, int) and jj == 0

                def exps(h):
                    hd = a * 2 + h
                    act.wait_ge(a_negmax, hd + 1)
                    for tb in range(TB):
                        p = PR[:, h, S_AT[tb]:S_AT[tb] + s_width(tb)]
                        act.activation(p, p, ACT.Exp, bias=NM[:, h, tb:tb + 1], scale=0.125,
                                       accum_out=DEN[:, h, tb:tb + 1]).then_inc(a_exp, 1)

                def copy_qk(n):
                    act.wait_ge(s_unit, (u + n).index + 1)
                    if not first:
                        act.wait_ge(a_qk, jj * 2 + n - 1)
                    act.copy(QC[:, n, :], B[n][:]).then_inc(a_copied, 1)

                def copy_probs(h):
                    hd = a * 2 + h
                    act.wait_ge(a_turned, hd * 3 + 2)
                    if not (isinstance(a, int) and a == 0):
                        act.wait_ge(a_pv, hd - 1)
                    act.copy(PT[:, h, 512:1024], B[6][:]).then_inc(a_pt_act, 1)

                if a is not None:
                    exps(0)
                if j is not None:
                    split_hi(act, u + 2, DC)
                    copy_qk(0)
                if a is not None:
                    copy_probs(0)
                if j is not None:
                    split_hi(act, u + 3, DC)
                    copy_qk(1)
                if a is not None:
                    exps(1)
                if j is not None:
                    split_hi(act, u + 4, DC)
                if a is not None:
                    copy_probs(1)
                if j is not None:
                    act.wait_ge(a_vt, jj + 1)
                    if first:
                        act.wait_ge(a_zero, 1)
                    if not (isinstance(jj, int) and jj < 2):
                        act.wait_ge(a_pv, jj * 2 - 2)
                    for h in range(2):
                        act.copy(VZ1[:, jp, h, :, 64 * h:64 * h + 64],
                                 B[0][:].rearrange("p (t d) -> p t d", t=TB)[:, :, 64 * h:64 * h + 64])\
                           .then_inc(a_v, 1)
                if a is not None:
                    act.wait_ge(a_pv, a * 2 + 2)
                    act.copy(M1H[:, a + POOL_TILES, :], B[7][:]).then_inc(s_m_hi, 1)

            attn_stage((0, 0), 0, None, None)
            for t in range(POOL_TILES):
                act.wait_ge(p_y, t + 1)
                if t:
                    act.wait_ge(p_m, t)
                act.activation(YT[:], B[5 + t][:], ACT.Copy, scale=GAINS[:, G_POOL + t:G_POOL + t + 1])\
                   .then_inc(p_yt, 1)
                act.wait_ge(p_yt, t + 1)
                act.copy(M1H[:, t, :], YT[:]).then_inc(p_hi, 1)
            attn_stage((1, 0), 1, 0, 0)
            with act.Fori(0, PAIRS1 // 2 - 1) as i:
                attn_stage((i * 2 + 2, i + 1), 0, i * 2 + 1, 1)
                attn_stage((i * 2 + 3, i + 1), 1, i * 2 + 2, 0)
            attn_stage(None, None, PAIRS1 - 1, 1)

            outputs(0, 1, U_OUT1, 1, DC, DC, gain_post=G_POST1)
            root(1)
            after_post(2, G_FFN1, 0)
            root(2, direct=True)
            ffn(0, U_FFN1, HALF)
            outputs(1, 3, U_DOWN1, 2, HALF, DC, gain_post=G_POSTF1)
            act.dma_start(CS2[:], ins["cos2"]).then_inc(r_tab, 16)
            act.dma_start(SN2[:], ins["sin2"]).then_inc(r_tab, 16)
            root(3)
            after_post(4, G_MIX2, DC)
            root(4, direct=True)

            def ret_head(h, last=False):
                def unit(n):
                    return Unit(U_RET + n, h, RET_UNITS)

                def copy_v(d, bank):
                    act.wait_ge(r_vt, h * RET_VT + d + 1)
                    act.copy(VT2[:, :, P * d:P * d + P], B[bank][:].rearrange("p (t d) -> p t d", t=TB))\
                       .then_inc(r_v, 1)

                def take_values(d, bank):
                    act.wait_ge(r_pv, h * RET_VT + d + 1)
                    act.copy(O2[:, d, :], B[bank][:]).then_inc(r_oc, 1)
                    if d >= 2:
                        act.wait_ge(r_acc, h * 3 + d - 1)
                    elif not (isinstance(h, int) and h == 0):
                        act.wait_ge(r_acc, h * 3)
                    act.activation(SQ[d % 2][:], B[bank][:], ACT.Square).then_inc(r_sq, 1)

                def silu(d):
                    act.wait_ge(r_g, h * RET_VT + d + 1)
                    act.activation(SG2[:, d, :], (TA if d % 2 == 0 else TC)[:], ACT.Silu).then_inc(r_sg, 1)

                if not (isinstance(h, int) and h == 0):
                    act.wait_ge(r_w, h * TB)
                act.dma_start(DECAY[:], ins["decay"][h]).then_inc(r_dec, 16)
                for n in range(5):
                    split_hi(act, unit(n + 2), DC)
                split_hi(act, unit(7), DC)
                copy_v(0, 0)
                split_hi(act, unit(8), DC)
                copy_v(1, 1)
                split_hi(act, unit(9), DC)
                copy_v(2, 2)
                split_hi(act, unit(10), DC)
                silu(0)
                copy_v(3, 3)
                take_values(0, 4)
                split_hi(act, unit(11), DC)
                silu(1)
                take_values(1, 5)
                split_hi(act, unit(12), DC)
                silu(2)
                take_values(2, 6)
                take_values(3, 4)
                split_hi(act, unit(13), DC)
                silu(3)
                act.wait_ge(r_mean, h + 1)
                act.activation(ACC[:], B[7][:], ACT.Sqrt, bias=EPSC, scale=D / (RET_VT * P)).then_inc(r_root, 1)
                for d in range(RET_VT):
                    act.wait_ge(r_p, h * RET_VT + d + 1)
                    act.copy(M2H[:, h * RET_VT + d, :], O2[:, d, :]).then_inc(s_m_hi, 1)

            ret_head(0)
            with act.Fori(1, RET_H) as h:
                ret_head(h)

            outputs(2, 5, U_RETO, 2, DC, DC, gain_next=G_FFN2)
            root(5)
            ffn(1, U_FFN2, HALF)
            outputs(3, 6, U_DOWN2, 2, HALF, DC, gain_next=G_MIX3)
            act.dma_start(MASK[:], ins["mask"]).then_inc(b_tab, 16)
            act.dma_start(TRI32[:], ins["tri"]).then_inc(b_tab, 16)
            act.dma_start(HEADMEAN[:], ins["headmean"]).then_inc(b_tab, 16)
            act.wait_ge(b_tab, 48)
            act.copy(LATER[:], TRI32[:, 0:P]).then_inc(b_tri, 1)
            act.copy(ALL[:], TRI32[:, P:2 * P]).then_inc(b_tri, 1)
            root(6)

            def stick_stage(j, jp, a, ap):
                u = None if j is None else Unit(U_SB + 3 * jp, j[1], 6)
                jj = None if j is None else j[0]
                first = isinstance(jj, int) and jj == 0

                def log_term(h):
                    hd = a * 2 + h
                    act.wait_ge(b_na, hd + 1)
                    act.activation(LG[:, h, :], LG[:, h, :], ACT.Exp).then_inc(b_lg, 1)
                    act.wait_ge(b_lg, hd * 2 + 1)
                    act.activation(LG[:, h, :], LG[:, h, :], ACT.Ln, bias=1.0).then_inc(b_lg, 1)

                def softplus_hi(h):
                    hd = a * 2 + h
                    act.wait_ge(b_sp, hd * 2 + 1)
                    if not (isinstance(a, int) and a == 0):
                        act.wait_ge(b_later, hd * 3 - 3)
                    act.copy(SPH[:, h, :], SP[:, h, :]).then_inc(b_hi, 1)

                def weights(h):
                    hd = a * 2 + h
                    act.wait_ge(b_arg, hd * 3 + 3)
                    act.activation(ZS[:, h, :], ZS[:, h, :], ACT.Exp).then_inc(b_w, 1)

                def squares(n):
                    act.wait_ge(b_qs, jj * 2 + n + 1)
                    if not first:
                        act.wait_ge(b_mean, jj * 2 + n - 1)
                    act.activation(SQ[n][:], QS[:, n, :], ACT.Square).then_inc(b_sq, 1)

                if a is not None:
                    log_term(0)
                if j is not None:
                    squares(0)
                    split_hi(act, u + 2, DC)
                if a is not None:
                    softplus_hi(0)
                if j is not None:
                    if a is not None:
                        log_term(1)
                    rn(0, jj, first)
                    squares(1)
                    split_hi(act, u + 3, DC)
                elif a is not None:
                    log_term(1)
                if a is not None:
                    softplus_hi(1)
                    weights(0)
                if j is not None:
                    rn(1, jj, first)
                    split_hi(act, u + 4, DC)
                if a is not None:
                    weights(1)
                if j is not None:
                    act.wait_ge(b_vt, jj + 1)
                    if first:
                        act.wait_ge(b_zero, 1)
                    if not (isinstance(jj, int) and jj < 2):
                        act.wait_ge(b_pv, jj * 2 - 2)
                    for h in range(2):
                        act.copy(VZ3[:, jp, h, :, 64 * h:64 * h + 64],
                                 B[1][:].rearrange("p (t d) -> p t d", t=TB)[:, :, 64 * h:64 * h + 64])\
                           .then_inc(b_v, 1)
                if a is not None:
                    act.wait_ge(b_pv, a * 2 + 2)
                    act.copy(M3H[:, a, :], B[7][:]).then_inc(s_m_hi, 1)

            def rn(n, jj, first):
                act.wait_ge(b_mean, jj * 2 + n + 1)
                if not first:
                    act.wait_ge(b_qk, jj * 2 + n - 1)
                act.activation(RQ[:, n, :], B[5 + n][:], ACT.Ln, bias=EPSC).then_inc(s_act, 1)
                act.wait_ge(s_act, jj * 2 + n + 1)
                act.activation(RQ[:, n, :], RQ[:, n, :], ACT.Exp, scale=-0.5).then_inc(b_rq, 1)

            stick_stage((0, 0), 0, None, None)
            stick_stage((1, 0), 1, 0, 0)
            with act.Fori(0, PAIRS3 // 2 - 1) as i:
                stick_stage((i * 2 + 2, i + 1), 0, i * 2 + 1, 1)
                stick_stage((i * 2 + 3, i + 1), 1, i * 2 + 2, 0)
            stick_stage(None, None, PAIRS3 - 1, 1)

            outputs(4, 7, U_OUT3, 1, DC, DC, gain_next=G_FFN3)
            root(7)
            ffn(2, U_FFN3, HALF)
            outputs(5, None, U_DOWN3, 2, HALF, 0)

        @block.vector
        def _(dve):
            steps = Steps(dve, s_dve)

            def zero_sum(n):
                dve.memset(ACC[:], 0.0).then_inc(s_zeroed, 1)

            def add_square(n, c, b):
                dve.wait_ge(s_squared, c + (8 * n + 1))
                dve.wait_ge(s_zeroed, SUMS[n])
                if not (n == 0 and isinstance(c, int) and c == 0):
                    dve.wait_ge(s_sq_used, c + 8 * n)
                dve.tensor_tensor(ACC[:], ACC[:], SQ[b][:], ALU.add).then_inc(s_sq_used, 1)

            def input_lo(which, c, g):
                dve.wait_ge(s_h_hi, c + (8 * which + 1))
                dve.scalar_tensor_tensor(out=HL[:, c, :], in0=X[:, c, :], scalar=gain(g, c),
                                         in1=HH[:, c, :].bitcast(F32), op0=ALU.mult,
                                         op1=ALU.subtract).then_inc(s_h, 1)

            def rnorm(n):
                dve.wait_ge(s_root, n + 1)
                dve.reciprocal(RB[:], ACC[:]).then_inc(s_rb, 1)
                dve.wait_ge(s_rb, n + 1)

            def ffn(f, u0):
                with dve.Fori(0, FC) as i:
                    wait_unit(dve, Unit(u0, i, 2))
                    dve.tensor_tensor(G1[:], B[0][:], RB[:], ALU.mult).then_inc(s_gate, 1)
                    wait_unit(dve, Unit(u0 + 1, i, 2))
                    dve.tensor_tensor(U1[:], B[1][:], RB[:], ALU.mult).then_inc(s_up, 1)
                    dve.wait_ge(s_silu, i + (FC * f + 1))
                    dve.wait_ge(s_up, i + (FC * f + 1))
                    dve.tensor_tensor(HD[:], SG[:], U1[:], ALU.mult).then_inc(s_hidden, 1)
                    dve.wait_ge(s_m_hi, i + (M_BASE[[1, 3, 5][f]] + 1))
                    dve.wait_ge(s_hidden, i + (FC * f + 1))
                    dve.tensor_tensor(ML[:, i, :], HD[:], MH[:, i, :].bitcast(F32), ALU.subtract).then_inc(s_m, 1)

            def outputs(o, n, u0, per, post, which=None, g=None):
                def two(i):
                    for b in range(2):
                        c = i * 2 + b
                        if not post:
                            wait_unit(dve, Unit(u0 + per * b + per - 1, i, 2 * per))
                            dve.tensor_tensor(X[:, c, :], X[:, c, :], B[b][:], ALU.add).then_inc(s_taken, 1)
                        if n is not None:
                            add_square(n, c, b)
                        if g is not None:
                            dve.wait_ge(s_taken, c + (8 * o + 1))
                            input_lo(which, c, g)
                if n is not None:
                    zero_sum(n)
                with dve.Fori(0, DC // 2) as i:
                    two(i)

            def after_post(base, which, g):
                for c in range(DC + 1):
                    if c < DC:
                        dve.tensor_tensor(F[:, c, :], F[:, c, :], RB[:], ALU.mult).then_inc(s_dve, 1)
                        dve.wait_ge(s_dve, steps.start + c + 1)
                        dve.tensor_tensor(X[:, c, :], X[:, c, :], F[:, c, :], ALU.add).then_inc(s_x_new, 1)
                    if c:
                        dve.wait_ge(s_x_new, base + c)
                        input_lo(which, c - 1, g)
                steps.end(DC)

            dve.wait_ge(s_x_in, 16 * (DC + 1))
            zero_sum(0)
            for c in range(DC):
                add_square(0, c, c % 2)
                input_lo(0, c, G_MIX1)
            rnorm(0)

            dve.wait_ge(a_zero, 4)
            dve.wait_ge(s_const, 16 * N_CONST)
            for t in range(POOL_TILES):
                dve.wait_ge(s_unit, t + 1)
                dve.tensor_tensor(UP[:, t, pad:], B[t][:], RB[:], ALU.mult).then_inc(p_u, 1)
            for tab in (CS1, SN1):
                steps.done(dve.tensor_tensor(tab[:], tab[:], RB[:], ALU.mult))
            steps.wait()
            steps.end()

            def attn_project(j, jp):
                jj = j[0]
                u = Unit(U_ATTN + 3 * jp, j[1], 6)

                def rotate(n):
                    dve.wait_ge(a_copied, jj * 2 + n + 1)
                    if not (isinstance(jj, int) and jj == 0):
                        dve.wait_ge(a_qk, jj * 2 + n)
                    steps.done(dve.tensor_tensor(RT[:, 0, :], QC[:, n, :], CS1[:], ALU.mult))
                    yield
                    dve.wait_ge(a_swapped, jj * 2 + n + 1)
                    steps.done(dve.tensor_tensor(RT[:, 1, :], B[n][:], SN1[:], ALU.mult))
                    steps.wait()
                    if not (isinstance(jj, int) and jj < 2):
                        dve.wait_ge(a_scores, jj * 2 - 2)
                    dve.tensor_tensor((QT1, KT1)[n][:, jp, :], RT[:, 0, :], RT[:, 1, :], ALU.add).then_inc(a_qk, 1)
                    yield

                def scale_v():
                    wait_unit(dve, u + 2)
                    if not (isinstance(jj, int) and jj == 0):
                        dve.wait_ge(a_vt, jj)
                    dve.tensor_tensor(V1[:], B[0][:], RB[:], ALU.mult).then_inc(a_vs, 1)
                return rotate, scale_v

            ATT_STEPS, PROJ_STEPS = 2, 4

            def attn_stage(j, jp, a, ap, between=()):
                if a is not None:
                    steps.at(a, ATT_STEPS + PROJ_STEPS)
                between = iter(between)

                def mask(h):
                    hd = a * 2 + h
                    dve.wait_ge(a_scores, hd + 1)
                    dve.sem_inc(a_mask_start, 1)
                    for tb, bank, at in ((3, 2, 0), (2, 3, 0), (0, 3, 384), (1, 4, 0)):
                        w = s_width(tb)
                        dve.tensor_tensor_reduce(PR[:, h, S_AT[tb]:S_AT[tb] + w], B[bank][:, at:at + w],
                                                 BIAS[:, T - w:T], 1.0, -3.0e38, ALU.add, ALU.max,
                                                 MX[:, h, tb:tb + 1]).then_inc(a_masked, 1)
                    dve.wait_ge(a_masked, hd * 4 + 4)
                    dve.tensor_scalar(NM[:, h, :], MX[:, h, :], -0.125, None, ALU.mult).then_inc(a_negmax, 1)

                def normalise(h):
                    hd = a * 2 + h
                    dve.wait_ge(a_exp, hd * 4 + 4)
                    steps.done(dve.reciprocal(RD[:, h, :], DEN[:, h, :]))
                    steps.wait()
                    for tb in range(TB):
                        p = PR[:, h, S_AT[tb]:S_AT[tb] + s_width(tb)]
                        dve.tensor_scalar(p, p, RD[:, h, tb:tb + 1], None, ALU.mult).then_inc(a_probs, 1)

                def copy_probs(h):
                    hd = a * 2 + h
                    if not (isinstance(a, int) and a == 0):
                        dve.wait_ge(a_pv, hd - 1)
                    dve.wait_ge(a_turned, hd * 3 + 1)
                    dve.tensor_copy(PT[:, h, 0:512], B[5][:]).then_inc(a_pt_dve, 1)
                    dve.wait_ge(a_turned, hd * 3 + 3)
                    dve.tensor_copy(PT[:, h, 1024:1280], B[4][:, 256:512]).then_inc(a_pt_dve, 1)

                if j is not None:
                    rotate, scale_v = attn_project(j, jp)
                    rq, rk = rotate(0), rotate(1)
                if a is not None:
                    mask(0)
                    normalise(0)
                if j is not None:
                    next(between, lambda: None)()
                    next(rq)
                if a is not None:
                    copy_probs(0)
                if j is not None:
                    next(rq)
                    next(between, lambda: None)()
                if a is not None:
                    mask(1)
                    normalise(1)
                if j is not None:
                    next(rk)
                    next(rk)
                    scale_v()
                if a is not None:
                    copy_probs(1)
                    dve.wait_ge(s_m_hi, a + 1)
                    dst = a + POOL_TILES
                    dve.tensor_tensor(M1L[:, dst, :], B[7][:], M1H[:, dst, :].bitcast(F32),
                                      ALU.subtract).then_inc(s_m, 1)

            PSTEP = sem("pool_steps")
            pn = [0]

            def pstep(ins):
                ins.then_inc(PSTEP, 1)
                pn[0] += 1
                dve.wait_ge(PSTEP, pn[0])

            def doubled(dst, src, by, rows=slice(0, P)):
                pstep(dve.tensor_tensor(dst[rows, pad:], src[rows, pad:], src[rows, pad - by:pad + T - by], ALU.add))

            dve.wait_ge(p_u, 2)
            def pools(t):
                doubled(WA, UP[:, t, :], 1)
                doubled(WB, WA, 2)
                if t:
                    doubled(WA, WB, 4)
                    doubled(WB, WA, 8)
                for r, w in ((slice(0, 64), WA), (slice(64, P), WB)):
                    pstep(dve.tensor_tensor(DF[r, t, :], w[r, pad:], INV[r, t, :], ALU.mult))
                dve.tensor_tensor(DF[:, t, :], DF[:, t, :], UP[:, t, pad:], ALU.subtract).then_inc(p_d, 1)

            attn_stage((0, 0), 0, None, None, between=(lambda: pools(0), lambda: pools(1)))
            steps.end()
            for t in range(POOL_TILES):
                dve.wait_ge(p_hi, t + 1)
                dve.tensor_tensor(M1L[:, t, :], YT[:], M1H[:, t, :].bitcast(F32), ALU.subtract).then_inc(p_m, 1)

            attn_stage((1, 0), 1, 0, 0)
            with dve.Fori(0, PAIRS1 // 2 - 1) as i:
                attn_stage((i * 2 + 2, i + 1), 0, i * 2 + 1, 1)
                attn_stage((i * 2 + 3, i + 1), 1, i * 2 + 2, 0)
            attn_stage(None, None, PAIRS1 - 1, 1)
            steps.end(PAIRS1 * ATT_STEPS + (PAIRS1 - 1) * PROJ_STEPS)

            outputs(0, 1, U_OUT1, 1, True)
            rnorm(1)
            after_post(0, 1, G_FFN1)
            rnorm(2)
            ffn(0, U_FFN1)
            outputs(1, 3, U_DOWN1, 2, True)
            rnorm(3)
            after_post(DC, 2, G_MIX2)
            rnorm(4)

            dve.wait_ge(r_tab, 32)
            dve.tensor_tensor(CS2[:], CS2[:], RB[:], ALU.mult).then_inc(r_cs, 1)
            dve.tensor_tensor(SN2[:], SN2[:], RB[:], ALU.mult).then_inc(r_cs, 1)
            dve.wait_ge(r_cs, 2)
            RET_STEPS = 2 * 3 + RET_VT

            def ret_head(h):
                steps.at(h, RET_STEPS)
                first = isinstance(h, int) and h == 0

                def unit(n):
                    return Unit(U_RET + n, h, RET_UNITS)

                def rotate(n, dst):
                    x1, x2 = B[2 * n][:], B[2 * n + 1][:]
                    wait_unit(dve, unit(2 * n))
                    steps.done(dve.tensor_tensor(TA[:], x1, CS2[:], ALU.mult))
                    steps.done(dve.tensor_tensor(dst[:, 1, :], x1, SN2[:], ALU.mult))
                    wait_unit(dve, unit(2 * n + 1))
                    steps.done(dve.tensor_tensor(TC[:], x2, SN2[:], ALU.mult))
                    steps.wait()
                    dve.tensor_tensor(dst[:, 0, :], TA[:], TC[:], ALU.subtract).then_inc(r_qk, 1)
                    dve.wait_ge(r_qk, h * 4 + 2 * n + 1)
                    dve.tensor_tensor(TA[:], x2, CS2[:], ALU.mult).then_inc(r_taken, 2)
                    dve.wait_ge(r_taken, h * TAKEN + (2 * n + 2))
                    dve.tensor_tensor(dst[:, 1, :], dst[:, 1, :], TA[:], ALU.add).then_inc(r_qk, 1)
                    dve.wait_ge(r_qk, h * 4 + 2 * n + 2)

                def scale(n, bank, dst, done):
                    wait_unit(dve, unit(n))
                    dve.tensor_tensor(dst[:], B[bank][:], RB[:], ALU.mult).then_inc(done, 1)

                def add_squares(d):
                    dve.wait_ge(r_sq, h * RET_VT + d + 1)
                    if d == 1:
                        dve.tensor_tensor(ACC[:], SQ[0][:], SQ[1][:], ALU.add).then_inc(r_acc, 1)
                    else:
                        dve.wait_ge(r_acc, h * 3 + d - 1)
                        dve.tensor_tensor(ACC[:], ACC[:], SQ[d % 2][:], ALU.add).then_inc(r_acc, 1)

                rotate(0, QT2)
                rotate(1, KT2)
                scale(4, 0, TA, r_taken)
                dve.wait_ge(r_dec, h * 16 + 16)
                if not first:
                    dve.wait_ge(r_pv, h * RET_VT)
                for n, (sb_, bank, at) in enumerate(((0, 4, 0), (1, 5, 0), (3, 5, 384), (2, 6, 0))):
                    w = t_width(sb_)
                    dve.wait_ge(r_sc, h * TB + (4 if n else 1))
                    dve.tensor_tensor(SC2[:, T_AT[sb_]:T_AT[sb_] + w], B[bank][:, at:at + w], DECAY[:, 0:w],
                                      ALU.mult).then_inc(r_w, 1)
                scale(5, 1, TC, r_taken)
                dve.wait_ge(r_vt, h * RET_VT + 1)
                scale(6, 2, TA, r_taken)
                dve.wait_ge(r_vt, h * RET_VT + 2)
                scale(7, 3, TC, r_taken)
                dve.wait_ge(r_vt, h * RET_VT + 3)
                scale(8, 0, TA, r_g)
                dve.wait_ge(r_vt, h * RET_VT + 4)
                scale(9, 1, TC, r_g)
                dve.wait_ge(r_sg, h * RET_VT + 1)
                add_squares(1)
                scale(10, 2, TA, r_g)
                dve.wait_ge(r_sg, h * RET_VT + 2)
                add_squares(2)
                add_squares(3)
                wait_unit(dve, unit(11))
                dve.tensor_tensor(TC[:], B[3][:], RB[:], ALU.mult).then_inc(r_g, 1)
                dve.wait_ge(r_root, h + 1)
                dve.reciprocal(ACC[:], ACC[:]).then_inc(r_ro, 1)
                dve.wait_ge(r_ro, h + 1)
                for d in range(RET_VT):
                    dve.wait_ge(r_oc, h * RET_VT + d + 1)
                    steps.done(dve.scalar_tensor_tensor(out=O2[:, d, :], in0=O2[:, d, :],
                                                        scalar=gain(G_RET, h * RET_VT + d), in1=ACC[:],
                                                        op0=ALU.mult, op1=ALU.mult))
                    dve.wait_ge(r_sg, h * RET_VT + d + 1)
                    steps.wait()
                    dve.tensor_tensor(O2[:, d, :], O2[:, d, :], SG2[:, d, :], ALU.mult).then_inc(r_p, 1)
                    if d:
                        lo(h, d - 1)
                lo(h, RET_VT - 1)

            def lo(h, d):
                t = h * RET_VT + d
                dve.wait_ge(s_m_hi, t + (M_BASE[2] + 1))
                dve.wait_ge(r_p, t + 1)
                dve.tensor_tensor(M2L[:, t, :], O2[:, d, :], M2H[:, t, :].bitcast(F32), ALU.subtract).then_inc(s_m, 1)

            ret_head(0)
            with dve.Fori(1, RET_H) as h:
                ret_head(h)
            steps.end(RET_H * RET_STEPS)

            outputs(2, 5, U_RETO, 2, False, 3, G_FFN2)
            rnorm(5)
            ffn(1, U_FFN2)
            outputs(3, 6, U_DOWN2, 2, False, 4, G_MIX3)
            rnorm(6)

            def stick_stage(j, jp, a, ap):
                u = None if j is None else Unit(U_SB + 3 * jp, j[1], 6)
                jj = None if j is None else j[0]
                first = isinstance(jj, int) and jj == 0

                def take_z(h):
                    hd = a * 2 + h
                    if not (isinstance(a, int) and a == 0):
                        dve.wait_ge(b_pv, hd - 1)
                    for n, (sb_, bank, at) in enumerate(((0, 2, 0), (1, 3, 0), (3, 3, 384), (2, 4, 0))):
                        w = t_width(sb_)
                        dve.wait_ge(b_z, hd * 4 + (4 if n else 1))
                        dve.scalar_tensor_tensor(out=ZS[:, h, T_AT[sb_]:T_AT[sb_] + w], in0=B[bank][:, at:at + w],
                                                 scalar=0.125, in1=MASK[:, 0:w], op0=ALU.mult,
                                                 op1=ALU.add).then_inc(b_zs, 1)
                    dve.wait_ge(b_zs, hd * 4 + 4)
                    dve.scalar_tensor_tensor(out=LG[:, h, :], in0=ZS[:, h, :], scalar=-1.0, in1=ZS[:, h, :],
                                             op0=ALU.mult, op1=ALU.min).then_inc(b_na, 1)

                def softplus(h):
                    hd = a * 2 + h
                    dve.wait_ge(b_lg, hd * 2 + 2)
                    dve.scalar_tensor_tensor(out=SP[:, h, :], in0=ZS[:, h, :], scalar=0.0, in1=LG[:, h, :],
                                             op0=ALU.max, op1=ALU.add).then_inc(b_sp, 1)
                    dve.scalar_tensor_tensor(out=ZS[:, h, :], in0=ZS[:, h, :], scalar=0.0, in1=LG[:, h, :],
                                             op0=ALU.min, op1=ALU.subtract).then_inc(b_sp, 1)

                def softplus_lo(h):
                    hd = a * 2 + h
                    dve.wait_ge(b_hi, hd + 1)
                    dve.tensor_tensor(SPL[:, h, :], SP[:, h, :], SPH[:, h, :].bitcast(F32),
                                      ALU.subtract).then_inc(b_lo, 1)

                def exponent(h):
                    hd = a * 2 + h
                    dve.wait_ge(b_sp, hd * 2 + 2)
                    for n, (bank, at, w) in enumerate(((2, 0, 512), (3, 512, 512), (4, 1024, 256))):
                        dve.wait_ge(b_later, hd * 3 + n + 1)
                        dve.tensor_tensor(ZS[:, h, at:at + w], ZS[:, h, at:at + w], B[bank][:, 0:w],
                                          ALU.subtract).then_inc(b_arg, 1)

                def scale_qk(n):
                    wait_unit(dve, u + n)
                    if not first:
                        dve.wait_ge(b_qk, jj * 2 + n - 1)
                    dve.tensor_tensor(QS[:, n, :], B[n][:], RB[:], ALU.mult).then_inc(b_qs, 1)

                def norm_qk(n):
                    dve.wait_ge(b_rq, jj * 2 + n + 1)
                    dve.wait_ge(b_qs, jj * 2 + n + 1)
                    if not (isinstance(jj, int) and jj < 2):
                        dve.wait_ge(b_z, jj * 8 - 8)
                    dve.scalar_tensor_tensor(out=(QT3, KT3)[n][:, jp, :], in0=QS[:, n, :],
                                             scalar=GAINS[:, G_Q + n:G_Q + n + 1], in1=RQ[:, n, :], op0=ALU.mult,
                                             op1=ALU.mult).then_inc(b_qk, 1)

                if a is not None:
                    take_z(0)
                if j is not None:
                    scale_qk(0)
                if a is not None:
                    softplus(0)
                    take_z(1)
                    softplus_lo(0)
                if j is not None:
                    norm_qk(0)
                    scale_qk(1)
                if a is not None:
                    softplus(1)
                    softplus_lo(1)
                    exponent(0)
                if j is not None:
                    norm_qk(1)
                    wait_unit(dve, u + 2)
                    if not first:
                        dve.wait_ge(b_vt, jj)
                    dve.tensor_tensor(V3[:], B[0][:], RB[:], ALU.mult).then_inc(b_vs, 1)
                if a is not None:
                    exponent(1)
                    dve.wait_ge(s_m_hi, a + (M_BASE[4] + 1))
                    dve.tensor_tensor(M3L[:, a, :], B[7][:], M3H[:, a, :].bitcast(F32), ALU.subtract).then_inc(s_m, 1)

            dve.wait_ge(b_tab, 48)
            stick_stage((0, 0), 0, None, None)
            stick_stage((1, 0), 1, 0, 0)
            with dve.Fori(0, PAIRS3 // 2 - 1) as i:
                stick_stage((i * 2 + 2, i + 1), 0, i * 2 + 1, 1)
                stick_stage((i * 2 + 3, i + 1), 1, i * 2 + 2, 0)
            stick_stage(None, None, PAIRS3 - 1, 1)

            outputs(4, 7, U_OUT3, 1, False, 5, G_FFN3)
            rnorm(7)
            ffn(2, U_FFN3)
            outputs(5, None, U_DOWN3, 2, False)


def tables():
    p, t = np.arange(P)[:, None], np.arange(T)[None, :]
    out = {"ident": np.eye(P), "mean": np.full((P, P), 1.0 / D)}

    swap = np.zeros((P, P))
    for m in range(P):
        swap[m ^ 32, m] = 1.0 if m & 32 else -1.0
    out["swap"] = swap

    def angles(half, index):
        freqs = np.power(np.float32(10000.0), (-(np.arange(half) / half)).astype(np.float32)).astype(np.float32)
        return (t.astype(np.float32) * freqs[index]).astype(np.float32).astype(np.float64)
    a1 = angles(32, p % 32)
    out["cos1"], out["sin1"] = np.cos(a1), np.sin(a1)
    a2 = angles(P, p)
    out["cos2"], out["sin2"] = np.cos(a2), np.sin(a2)

    dist = T - P + p - t
    branches = ((dist >= 0) & (dist <= P)).astype(int)
    for dilation in (4, 16):
        branches += (dist >= 0) & (dist % dilation == 0)
    out["bias"] = np.where(branches > 0, 8.0 * np.log(np.maximum(branches, 1)), -1e30)

    gamma = 1.0 - 2.0 ** (-5.0 - np.arange(RET_H))
    seen = (t // 64) >= (p // 64)
    out["decay"] = np.stack([np.where(seen, g ** np.abs(t - p) / 16.0, 0.0) for g in gamma])
    out["mask"] = np.where(t > p, 0.0, -1e30)
    q = np.arange(P)[None, :]
    out["tri"] = np.concatenate([(p > q).astype(float), np.ones((P, P))], axis=1)
    out["headmean"] = np.where(p // 64 == q // 64, 1.0 / 64, 0.0)

    windows = np.array([[2, 8], [4, 16]])
    out["inv_counts"] = np.stack([1.0 / np.minimum(t + 1, windows[p // 64, n]) for n in range(POOL_TILES)], axis=1)
    return {k: np.ascontiguousarray(v, np.float32) for k, v in out.items()}


def unit_tiles(w):
    k, n = w.shape
    return w.reshape(k // P, P, n // P, P).transpose(2, 1, 0, 3)


def halves(tiles):
    n, _, k, _ = tiles.shape
    return tiles.reshape(n, P, 2, k // 2, P).transpose(0, 2, 1, 3, 4).reshape(2 * n, P, k // 2, P)


def interleaved(*parts):
    return np.stack(parts, axis=1).reshape(-1, *parts[0].shape[1:])


def layout(i):
    w_in = unit_tiles(i["w_in"][0])
    q, k, v = (w_in[POOL_TILES + PAIRS1 * n:POOL_TILES + PAIRS1 * (n + 1)] for n in range(3))
    ret = unit_tiles(i["ret_w_in_2"][0])
    nq, nv = RET_H * RET_QT, RET_H * RET_VT
    ret_order = []
    for h in range(RET_H):
        for base, per in ((0, RET_QT), (nq, RET_QT), (2 * nq, RET_VT), (2 * nq + nv, RET_VT)):
            ret_order += [base + per * h + n for n in range(per)]
    sb = unit_tiles(i["sb_w_in_2"][0])
    ffn = [unit_tiles(i["ffn_w_in_2"][n]) for n in range(2)]
    small = [
        w_in[:POOL_TILES], interleaved(q, k, v), unit_tiles(i["w_out"][0]),
        interleaved(unit_tiles(i["w_gate"][0]), unit_tiles(i["w_up"][0])),
        ret[ret_order], halves(unit_tiles(i["ret_w_o_2"][0])), interleaved(ffn[0][:FC], ffn[0][FC:]),
        interleaved(*(sb[PAIRS3 * n:PAIRS3 * (n + 1)] for n in range(3))), unit_tiles(i["sb_w_o_2"][0]),
        interleaved(ffn[1][:FC], ffn[1][FC:]),
    ]
    large = [halves(unit_tiles(w)) for w in (i["w_down"][0], i["ffn_w_out_2"][0], i["ffn_w_out_2"][1])]
    cols = [i[n].reshape(DC, P).T for n in ("ln_pre_mix", "ln_post_mix", "ln_pre_ffn", "ln_post_ffn")]
    for n in range(2):
        cols += [i["mix_norm_2"][n].reshape(DC, P).T, i["ffn_norm_2"][n].reshape(DC, P).T]
    cols.append(i["pool_scale"][0].reshape(POOL_TILES, P).T)
    cols.append(i["ret_out_norm_2"][0].reshape(RET_H * RET_VT, P).T)
    for n in ("sb_q_norm_2", "sb_k_norm_2"):
        cols.append(np.tile(i[n][0], 2)[:, None])
    cols.append(np.full((P, 1), EPS, np.float32))
    w_pool = np.zeros((P, POOL_TILES, P), np.float32)
    for g in range(2 * POOL_TILES):
        r = slice(64 * (g % 2), 64 * (g % 2) + 64)
        w_pool[r, g // 2, r] = i["w_pool"][0, g]
    return {
        "x_t": i["x"][0].T.reshape(DC, P, T).transpose(1, 0, 2),
        "w_small": np.concatenate(small).reshape(-1, P, DC * P),
        "w_large": np.concatenate(large).reshape(-1, P, HALF * P),
        "gains": np.concatenate(cols, axis=1),
        "w_pool": w_pool,
    }


def kernel(**inputs):
    import concourse.bacc as bacc
    from concourse.bass_utils import run_bass_kernel_spmd

    nc = bacc.Bacc("TRN2", target_bir_lowering=False, num_devices=1)
    arrays = layout({k: np.asarray(v) for k, v in inputs.items()}) | tables()
    arrays = {f"in_{k}": np.ascontiguousarray(v) for k, v in arrays.items()}
    ins = {k.removeprefix("in_"): nc.dram_tensor(k, a.shape, mybir.dt.from_np(a.dtype), kind="ExternalInput").ap()
           for k, a in arrays.items()}
    out_t = nc.dram_tensor("out_t", (P, DC, T), F32, kind="ExternalOutput").ap()
    build(nc, ins, out_t)
    r = run_bass_kernel_spmd(nc, [arrays], core_ids=[0])
    got = np.asarray(r.results[0]["out_t"])
    return np.ascontiguousarray(got.transpose(2, 1, 0).reshape(1, T, D))
```

```python
from contextlib import ExitStack

import numpy as np

import concourse.bass as bass
from concourse import mybir

P = 128
T = 512
D = 1024
DC = D // P
FF = 2816
FC = FF // P
HALF = FC // 2
POOL_TILES = 2
PAIRS1 = 6
RET_H, RET_QT, RET_VT = 4, 2, 4
PAIRS3 = 8
TB = T // P
EPS = 1e-6

ALU = mybir.AluOpType
ACT = mybir.ActivationFunctionType
F32 = mybir.dt.float32
F32R = mybir.dt.float32r
LOG_EXP = "natural_log_exp_and_others"

U_POOL = 0
U_ATTN = U_POOL + POOL_TILES
U_OUT1 = U_ATTN + 3 * PAIRS1
U_FFN1 = U_OUT1 + DC
U_DOWN1 = U_FFN1 + 2 * FC
U_RET = U_DOWN1 + 2 * DC
RET_UNITS = 2 * RET_QT + 2 * RET_VT
U_RETO = U_RET + RET_H * RET_UNITS
U_FFN2 = U_RETO + 2 * DC
U_DOWN2 = U_FFN2 + 2 * FC
U_SB = U_DOWN2 + 2 * DC
U_OUT3 = U_SB + 3 * PAIRS3
U_FFN3 = U_OUT3 + DC
U_DOWN3 = U_FFN3 + 2 * FC
U_END = U_DOWN3 + 2 * DC
STRETCHES = [(U_DOWN1, DC, False), (2 * DC, HALF, True), (U_DOWN2 - U_RET, DC, False), (2 * DC, HALF, True),
             (U_DOWN3 - U_SB, DC, False), (2 * DC, HALF, True)]

G_MIX1, G_POST1, G_FFN1, G_POSTF1, G_MIX2, G_FFN2, G_MIX3, G_FFN3 = (DC * n for n in range(8))
G_POOL = 8 * DC
G_RET = G_POOL + POOL_TILES
G_Q = G_RET + RET_H * RET_VT
G_K = G_Q + 1
G_EPS = G_K + 1
G_COLS = G_EPS + 1

WIDE = 1280
T_AT = [0, 512, 1024, 896]
S_AT = [896, 1024, 512, 0]


def t_width(block):
    return T - P * block


def s_width(block):
    return P * (block + 1)


class Unit:

    def __init__(self, first, i=0, step=0):
        assert step % 2 == 0
        self.s = first % 2
        self.m = i * (step // 2) + first // 2 if step else first // 2
        self.first = first

    def __add__(self, n):
        u = Unit(self.first + n)
        u.m = self.m + ((self.first + n) // 2 - self.first // 2)
        return u

    @property
    def index(self):
        return self.m * 2 + self.s


class Steps:

    def __init__(self, eng, sem):
        self.eng, self.sem, self.base, self.n, self.start = eng, sem, 0, 0, 0

    def at(self, index, per, but=0):
        self.n = 0
        self.base = index * per + (self.start - but)

    def end(self, count=None):
        self.start += self.n if count is None else count
        self.base, self.n = self.start, 0

    def done(self, ins):
        ins.then_inc(self.sem, 1)
        self.n += 1

    def wait(self, back=0):
        self.eng.wait_ge(self.sem, self.base + self.n - back)


def build(nc, ins, out_t):
    ctx = ExitStack()
    with ctx:
        def alloc(stack, name, shape, dt=F32):
            return stack.enter_context(nc.sbuf_tensor(name, shape, dt))

        def sb(name, shape, dt=F32):
            return alloc(ctx, name, shape, dt)

        def sem(name):
            return ctx.enter_context(nc.semaphore(name))

        X = sb("X", [P, DC, T])
        HH = sb("HH", [P, DC, T], F32R)
        HL = sb("HL", [P, DC, T], F32R)
        RAW = [sb(f"RAW{s}", [P, HALF, P]) for s in range(2)]
        WH = [sb(f"WH{s}", [P, HALF, P], F32R) for s in range(2)]
        WL = [sb(f"WL{s}", [P, HALF, P], F32R) for s in range(2)]
        RB = sb("RB", [P, T])
        ACC = sb("ACC", [P, T])
        SQ = [sb(f"SQ{s}", [P, T]) for s in range(2)]
        GAINS = sb("GAINS", [P, G_COLS])
        RBT = sb("RBT", [P, TB])
        IDENT = sb("IDENT", [P, P])
        MEAN = sb("MEAN", [P, P])

        def scratch(tensors):
            with ExitStack() as stack:
                return [alloc(stack, *t) for t in tensors]

        MH, ML, G1, SG, U1, HD, F = scratch([
            ("MH", [P, FC, T], F32R), ("ML", [P, FC, T], F32R), ("G1", [P, T]), ("SG", [P, T]),
            ("U1", [P, T]), ("HD", [P, T]), ("F", [P, DC, T])])
        pad = 16
        (M1H, M1L, QT1, KT1, VZ1, QC, RT, PR, PT, BIAS, CS1, SN1, SWAP, V1, MX, NM, DEN, RD,
         UP, WA, WB, INV, DF, YT, WPOOL) = scratch([
             ("M1H", [P, DC, T], F32R), ("M1L", [P, DC, T], F32R), ("QT1", [P, 2, T]), ("KT1", [P, 2, T]),
             ("VZ1", [P, 2, 2, TB, P]), ("QC", [P, 2, T]), ("RT", [P, 2, T]), ("PR", [P, 2, WIDE]),
             ("PT", [P, 2, WIDE]), ("BIAS", [P, T]), ("CS1", [P, T]), ("SN1", [P, T]), ("SWAP", [P, P]),
             ("V1", [P, T]), ("MX", [P, 2, TB]), ("NM", [P, 2, TB]), ("DEN", [P, 2, TB]), ("RD", [P, 2, TB]),
             ("UP", [P, POOL_TILES, pad + T]), ("WA", [P, pad + T]), ("WB", [P, pad + T]),
             ("INV", [P, POOL_TILES, T]), ("DF", [P, POOL_TILES, T]), ("YT", [P, T]), ("WPOOL", [P, POOL_TILES, P])])
        M2H, M2L, CS2, SN2, DECAY, QT2, KT2, SC2, VT2, O2, SG2, TA, TC = scratch([
            ("M2H", [P, RET_H * RET_VT, T], F32R), ("M2L", [P, RET_H * RET_VT, T], F32R), ("CS2", [P, T]),
            ("SN2", [P, T]), ("DECAY", [P, T]), ("QT2", [P, RET_QT, T]), ("KT2", [P, RET_QT, T]), ("SC2", [P, WIDE]),
            ("VT2", [P, TB, T]), ("O2", [P, RET_VT, T]), ("SG2", [P, RET_VT, T]), ("TA", [P, T]), ("TC", [P, T])])
        (M3H, M3L, QT3, KT3, VZ3, QS, V3, RQ, ZS, LG, SP, SPH, SPL, MASK, TRI32, LATER, ALL, HEADMEAN) = scratch([
            ("M3H", [P, DC, T], F32R), ("M3L", [P, DC, T], F32R), ("QT3", [P, 2, T]), ("KT3", [P, 2, T]),
            ("VZ3", [P, 2, 2, TB, P]), ("QS", [P, 2, T]), ("V3", [P, T]), ("RQ", [P, 2, T]), ("ZS", [P, 2, WIDE]),
            ("LG", [P, 2, WIDE]), ("SP", [P, 2, WIDE]), ("SPH", [P, 2, WIDE], F32R), ("SPL", [P, 2, WIDE], F32R),
            ("MASK", [P, T]), ("TRI32", [P, 2 * P]), ("LATER", [P, P], F32R), ("ALL", [P, P], F32R),
            ("HEADMEAN", [P, P])])

        CONSTS = [(IDENT[:], "ident"), (MEAN[:], "mean"), (BIAS[:], "bias"), (CS1[:], "cos1"), (SN1[:], "sin1"),
                  (SWAP[:], "swap"), (INV[:], "inv_counts"), (WPOOL[:], "w_pool")]
        N_CONST = len(CONSTS)
        SUMS = {0: 1, 1: 2, 3: 3, 5: 4, 6: 5, 7: 6}

        B = [ctx.enter_context(nc.psum_tensor(f"B{n}", [P, T], F32)) for n in range(8)]

        s_raw = [sem(f"raw_landed{s}") for s in range(2)]
        s_hi = sem("weights_hi")
        s_lo = sem("weights_lo")
        s_hi_used = sem("weights_hi_used")
        s_unit = sem("unit_done")
        s_warm = sem("warm_up_zeroed")
        X_PARTS = DC // 2
        s_x_in = [sem(f"x_landed{g}") for g in range(X_PARTS)]
        s_gains = sem("gains_landed")
        s_const = sem("constants_landed")
        s_squared = sem("squared")
        s_sq_used = sem("square_added")
        s_zeroed = sem("sum_zeroed")
        s_mean = sem("mean_ready")
        s_root = sem("root_ready")
        s_rb = sem("rnorm_ready")
        s_h_hi = sem("input_hi")
        s_h = sem("input_ready")
        s_taken = sem("tile_taken")
        s_f0 = sem("first_tile_scaled")
        s_f = sem("tile_scaled")
        s_x_new = sem("x_updated")
        s_out = sem("output_stored")
        s_gate = sem("gate_scaled")
        s_silu = sem("silu_done")
        s_up = sem("up_scaled")
        s_hidden = sem("hidden_done")
        s_m_hi = sem("mixed_hi")
        s_m = sem("mixed_ready")
        s_dve = sem("vector_steps")
        s_act = sem("scalar_steps")

        def gain(base, c):
            return GAINS[:, bass.ds(c + base, 1)]

        def wait_unit(eng, u):
            eng.wait_ge(s_unit, u.index + 1)

        def split_hi(act, u, chunks):
            if not chunks:
                return
            act.wait_ge(s_raw[u.s], u.m * 16 + 16)
            if not (isinstance(u.m, int) and u.index < 2):
                act.wait_ge(s_hi_used, u.index - 1)
            act.copy(WH[u.s][:, 0:chunks, :], RAW[u.s][:, 0:chunks, :]).then_inc(s_hi, 1)

        def use_unit(pe, u, bank, chunks, xh, xl, k0=0, start=True, stop=True, before=None):
            if before is not None:
                start_unit(pe, u, bank, chunks, xh, xl, before, k0, start)
                finish_unit(pe, u, bank, chunks, xh, xl, before, k0, stop)
                return
            wh, wl = WH[u.s], WL[u.s]
            pe.wait_ge(s_hi, u.index + 1)
            for c in range(chunks):
                pe.matmul(bank, wh[:, c, :], xh[:, k0 + c, :], start=(start and c == 0), stop=False)
                mm = pe.matmul(bank, wh[:, c, :], xl[:, k0 + c, :], start=False, stop=False)
            mm.then_inc(s_hi_used, 1)
            pe.wait_ge(s_lo, u.index + 1)
            for c in range(chunks):
                mm = pe.matmul(bank, wl[:, c, :], xh[:, k0 + c, :], start=False,
                               stop=(stop and c == chunks - 1))
            mm.then_inc(s_unit, 1)

        def start_unit(pe, u, bank, chunks, xh, xl, before, k0=0, start=True):
            wh, wl = WH[u.s], WL[u.s]
            pe.wait_ge(s_hi, u.index + 1)
            pe.wait_ge(s_lo, u.index + 1)
            for c in range(chunks - 1):
                before(k0 + c)
                pe.matmul(bank, wh[:, c, :], xh[:, k0 + c, :], start=(start and c == 0), stop=False)
                pe.matmul(bank, wh[:, c, :], xl[:, k0 + c, :], start=False, stop=False)
                pe.matmul(bank, wl[:, c, :], xh[:, k0 + c, :], start=False, stop=False)

        def finish_unit(pe, u, bank, chunks, xh, xl, before, k0=0, stop=True):
            wh, wl, c = WH[u.s], WL[u.s], chunks - 1
            before(k0 + c)
            pe.matmul(bank, wh[:, c, :], xh[:, k0 + c, :], start=False, stop=False)
            pe.matmul(bank, wh[:, c, :], xl[:, k0 + c, :], start=False, stop=False).then_inc(s_hi_used, 1)
            pe.matmul(bank, wl[:, c, :], xh[:, k0 + c, :], start=False, stop=stop).then_inc(s_unit, 1)

        block = ctx.enter_context(nc.Block())

        M_BASE = [0, PAIRS1, PAIRS1 + FC, PAIRS1 + FC + 16, PAIRS1 + 2 * FC + 16, PAIRS1 + 2 * FC + 16 + PAIRS3]

        a_copied = sem("a_qk_copied")
        a_swapped = sem("a_qk_swapped")
        a_qk = sem("a_qk_ready")
        a_vs = sem("a_v_scaled")
        a_vt = sem("a_v_turned")
        a_v = sem("a_v_ready")
        a_scores = sem("a_scores_ready")
        a_mask_start = sem("a_masking_started")
        a_masked = sem("a_scores_masked")
        a_negmax = sem("a_negmax_ready")
        a_exp = sem("a_exp_done")
        a_probs = sem("a_probs_ready")
        a_turned = sem("a_probs_turned")
        a_pt_act = sem("a_probs_copied_scalar")
        a_pt_dve = sem("a_probs_copied_vector")
        a_pv = sem("a_values_summed")
        a_zero = sem("a_zeroed")
        p_u = sem("p_u_ready")
        p_d = sem("p_differences_ready")
        p_y = sem("p_products_ready")
        p_yt = sem("p_scaled")
        p_hi = sem("p_hi")
        p_m = sem("p_ready")
        r_tab = sem("r_tables_landed")
        r_dec = sem("r_decay_landed")
        r_cs = sem("r_tables_scaled")
        r_qk = sem("r_qk_ready")
        r_taken = sem("r_bank_taken")
        r_sc = sem("r_scores_ready")
        r_w = sem("r_scores_weighted")
        r_turned = sem("r_factors_turned")
        r_rbt = sem("r_factors_copied")
        r_v = sem("r_v_ready")
        r_g = sem("r_gate_scaled")
        r_sg = sem("r_gate_silu")
        r_pv = sem("r_values_summed")
        r_oc = sem("r_values_copied")
        r_sq = sem("r_squared")
        r_acc = sem("r_squares_added")
        r_mean = sem("r_mean_ready")
        r_root = sem("r_root_ready")
        r_ro = sem("r_rnorm_ready")
        r_p = sem("r_products_ready")
        b_tab = sem("b_tables_landed")
        b_tri = sem("b_tables_copied")
        b_qs = sem("b_qk_scaled")
        b_sq = sem("b_qk_squared")
        b_mean = sem("b_qk_mean")
        b_rq = sem("b_qk_rnorm")
        b_qk = sem("b_qk_ready")
        b_vs = sem("b_v_scaled")
        b_vt = sem("b_v_turned")
        b_v = sem("b_v_ready")
        b_z = sem("b_z_ready")
        b_zs = sem("b_z_copied")
        b_na = sem("b_negabs_ready")
        b_lg = sem("b_log_ready")
        b_sp = sem("b_softplus_ready")
        b_hi = sem("b_softplus_hi")
        b_lo = sem("b_softplus_lo")
        b_later = sem("b_later_ready")
        b_arg = sem("b_exponent_ready")
        b_w = sem("b_weights_ready")
        b_pv = sem("b_values_summed")
        b_zero = sem("b_zeroed")

        TAKEN = 4
        SUM_BANKS = (0, 4, 5, 6)

        @block.sync
        def _(sp):
            def load_unit(u, source, chunks):
                if not (isinstance(u.m, int) and u.index < 2):
                    sp.wait_ge(s_lo, u.index - 1)
                sp.dma_start(RAW[u.s][:, 0:chunks, :], source).then_inc(s_raw[u.s], 16)

            sp.dma_start(GAINS[:], ins["gains"]).then_inc(s_gains, 16)
            at = {False: 0, True: 0}
            first = 0
            for count, chunks, large in STRETCHES:
                stream = ins["w_large" if large else "w_small"].rearrange("u p (c n) -> u p c n", c=chunks)
                start = 0
                if first == 0:
                    for n in range(2):
                        load_unit(Unit(n), stream[n], chunks)
                    for dst, name in CONSTS:
                        sp.dma_start(dst, ins[name]).then_inc(s_const, 16)
                    start = 1
                with sp.Fori(start, count // 2) as i:
                    for n in range(2):
                        load_unit(Unit(first + n, i, 2), stream[i * 2 + (at[large] + n)], chunks)
                first += count
                at[large] += count
            for c in range(DC):
                sp.wait_ge(s_taken, 8 * 5 + c + 1)
                sp.dma_start(out_t[:, c, :], X[:, c, :]).then_inc(s_out, 16)
            sp.wait_ge(s_out, 16 * DC)

        @block.gpsimd
        def _(pool):
            def split_lo(u, chunks):
                pool.wait_ge(s_hi, u.index + 1)
                if not (isinstance(u.m, int) and u.index < 2):
                    pool.wait_ge(s_unit, u.index - 1)
                pool.tensor_tensor(WL[u.s][:, 0:chunks, :], RAW[u.s][:, 0:chunks, :],
                                   WH[u.s][:, 0:chunks, :].bitcast(F32), ALU.subtract).then_inc(s_lo, 1)

            pool.memset(RB[:], 0.0).then_inc(s_warm, 1)
            pool.memset(VZ1[:], 0.0).then_inc(a_zero, 1)
            pool.memset(UP[:], 0.0).then_inc(a_zero, 1)
            pool.memset(WA[:], 0.0).then_inc(a_zero, 1)
            pool.memset(WB[:], 0.0).then_inc(a_zero, 1)
            def scale_f(n):
                pool.wait_ge(s_rb, n + 1)
                for c in range(1, DC):
                    pool.tensor_tensor(F[:, c, :], F[:, c, :], RB[:], ALU.mult).then_inc(s_f, 1)

            first = 0
            cuts = [(U_FFN1 + 2, DC), (U_DOWN1 - U_FFN1 - 2, DC), (U_RET - U_DOWN1, HALF), (2, DC)]
            stretches = cuts + [(STRETCHES[2][0] - 2, DC), (U_SB - U_DOWN2, HALF), (2, DC), (U_DOWN3 - U_SB - 2, DC),
                                (U_END - U_DOWN3, HALF)]
            for count, chunks in stretches:
                start = 0
                if first == 0:
                    for n in range(2):
                        split_lo(Unit(n), chunks)
                    start = 1
                if first == U_FFN1 + 2:
                    scale_f(1)
                if first == U_RET + 2:
                    scale_f(3)
                if first == U_SB + 2:
                    pool.wait_ge(s_unit, U_SB)
                    pool.memset(VZ3[:], 0.0).then_inc(b_zero, 1)
                with pool.Fori(start, count // 2) as i:
                    for n in range(2):
                        split_lo(Unit(first + n, i, 2), chunks)
                first += count

        @block.tensor
        def _(pe):
            def mean_of_sum(n):
                pe.wait_ge(s_sq_used, 8 * n + 8)
                pe.matmul(B[7][:], MEAN[:], ACC[:], start=True, stop=True).then_inc(s_mean, 1)

            def ready_h(which):
                return lambda k: pe.wait_ge(s_h, 8 * which + k + 1)

            def ready_h_and_mean(which, n):
                def before(k):
                    pe.wait_ge(s_squared, 8 * n + k + 1)
                    pe.matmul(B[7][:], MEAN[:], SQ[k % 2][:], start=(k == 0), stop=(k == DC - 1),
                              skip_group_check=True).then_inc(s_sq_used, 1)
                    pe.wait_ge(s_h, 8 * which + k + 1)
                return before

            def ffn(f, u0, before, n=None):
                def pair(i, before=None):
                    if before is None:
                        pe.wait_ge(s_gate, i + FC * f)
                    use_unit(pe, Unit(u0, i, 2), B[0][:], DC, HH, HL, before=before)
                    if before is not None and n is not None:
                        mean_of_sum(n)
                    if before is None:
                        pe.wait_ge(s_up, i + FC * f)
                    use_unit(pe, Unit(u0 + 1, i, 2), B[1][:], DC, HH, HL)
                pair(0, before)
                with pe.Fori(1, FC) as i:
                    pair(i)

            def outputs(o, u0, per, chunks, xh, xl, before, started=False):
                def two(i, before=None):
                    for b in range(2):
                        if before is None:
                            pe.wait_ge(s_taken, i * 2 + (8 * o + b - 1))
                        for q in range(per):
                            use_unit(pe, Unit(u0 + per * b + q, i, 2 * per), B[b][:], chunks, xh, xl,
                                     k0=chunks * q, start=(q == 0), stop=(q == per - 1),
                                     before=before if b == 0 else None)
                if started:
                    for b in range(2):
                        finish_unit(pe, Unit(u0 + b), B[b][:], chunks, xh, xl, before)
                else:
                    two(0, before)
                with pe.Fori(1, DC // 2) as i:
                    two(i)

            def ready_m1(k):
                if k >= POOL_TILES:
                    pe.wait_ge(s_m, k - POOL_TILES + 1)

            def start_out(b):
                if b == 0:
                    pe.wait_ge(a_v, 2 * PAIRS1)
                else:
                    pe.wait_ge(a_qk, 2 * PAIRS1)
                start_unit(pe, Unit(U_OUT1 + b), B[b][:], DC, M1H, M1L, ready_m1)

            def attn_stage(j, jp, a, ap):
                u = None if j is None else Unit(U_ATTN + 3 * jp, j[1], 6)
                jj = None if j is None else j[0]

                def scores(h):
                    hd = a * 2 + h
                    pe.wait_ge(a_qk, a * 2 + 2)
                    if not (isinstance(a, int) and a * 2 + h == 0):
                        pe.wait_ge(a_masked, hd * 4)
                        pe.wait_ge(a_pt_dve, hd * 2)
                    r = slice(64 * h, 64 * h + 64)
                    for tb, (bank, at) in ((3, (2, 0)), (2, (3, 0)), (0, (3, 384)), (1, (4, 0))):
                        w = s_width(tb)
                        mm = pe.matmul(B[bank][:, at:at + w], QT1[r, ap, P * tb:P * tb + P], KT1[r, ap, 0:w],
                                       start=True, stop=True)
                    mm.then_inc(a_scores, 1)

                def turn(h):
                    hd = a * 2 + h
                    pe.wait_ge(a_probs, hd * 4 + 4)
                    if isinstance(a, int) and a * 2 + h == 0:
                        pe.wait_ge(p_yt, POOL_TILES)
                    else:
                        pe.wait_ge(a_pt_act, hd)
                        pe.wait_ge(a_pt_dve, hd * 2)
                    for blocks in (((0, 5, 0),), ((1, 6, 0), (3, 6, 384)), ((2, 4, 256),)):
                        for sb_, bank, at in blocks:
                            for tb in range(sb_, TB):
                                col = S_AT[tb] + P * sb_
                                o = at + P * (tb - sb_)
                                mm = pe.transpose(B[bank][:, o:o + P], PR[:, h, col:col + P], IDENT[:])
                        mm.then_inc(a_turned, 1)

                def values(h, a, ap):
                    hd = a * 2 + h
                    pe.wait_ge(a_pt_act, hd + 1)
                    pe.wait_ge(a_pt_dve, hd * 2 + 2)
                    if h == 0:
                        pe.wait_ge(a_v, a * 2 + 2)
                        if not (isinstance(a, int) and a == 0):
                            pe.wait_ge(s_m, a)
                    for sb_ in range(TB):
                        w = t_width(sb_)
                        mm = pe.matmul(B[7][:, P * sb_:T], VZ1[:, ap, h, sb_, :],
                                       PT[:, h, T_AT[sb_]:T_AT[sb_] + w], start=(h == 0 and sb_ == 0),
                                       stop=(h == 1 and sb_ == TB - 1), skip_group_check=True)
                    mm.then_inc(a_pv, 1)

                def swap(n):
                    pe.wait_ge(a_copied, jj * 2 + n + 1)
                    pe.matmul(B[n][:], SWAP[:], QC[:, n, :], start=True, stop=True).then_inc(a_swapped, 1)

                first = isinstance(jj, int) and jj == 0
                if a is not None:
                    scores(0)
                if j is not None:
                    if not first:
                        pe.wait_ge(a_v, jj * 2)
                    else:
                        pe.wait_ge(p_u, 1)
                    use_unit(pe, u, B[0][:], DC, HH, HL)
                if a is not None:
                    if not (isinstance(a, int) and a == 0):
                        values(1, a - 1, 1 - ap)
                    if j is None:
                        start_out(0)
                    turn(0)
                if j is not None:
                    if not first:
                        pe.wait_ge(a_qk, jj * 2)
                    else:
                        pe.wait_ge(p_u, 2)
                    use_unit(pe, u + 1, B[1][:], DC, HH, HL)
                    swap(0)
                if a is not None:
                    scores(1)
                    if j is None:
                        start_out(1)
                    values(0, a, ap)
                if j is not None:
                    swap(1)
                    pe.wait_ge(a_qk, jj * 2 + 1)
                    use_unit(pe, u + 2, B[0][:], DC, HH, HL)
                if a is not None:
                    turn(1)
                if j is not None:
                    pe.wait_ge(a_vs, jj + 1)
                    for tb in range(TB):
                        mm = pe.transpose(B[0][:, P * tb:P * tb + P], V1[:, P * tb:P * tb + P], IDENT[:])
                    mm.then_inc(a_vt, 1)
                elif a is not None:
                    values(1, a, ap)

            pe.wait_ge(s_warm, 1)
            for _ in range(5):
                pe.matmul(B[7][:], RB[:, 0:P], RB[:], start=True, stop=True)
            use_unit(pe, Unit(0), B[0][:], DC, HH, HL, before=ready_h(0))
            pe.wait_ge(s_const, 16 * N_CONST)
            mean_of_sum(0)
            use_unit(pe, Unit(1), B[1][:], DC, HH, HL)
            attn_stage((0, 0), 0, None, None)
            for t in range(POOL_TILES):
                pe.wait_ge(p_d, t + 1)
                pe.matmul(B[5 + t][:], WPOOL[:, t, :], DF[:, t, :], start=True, stop=True).then_inc(p_y, 1)
            attn_stage((1, 0), 1, 0, 0)
            with pe.Fori(0, PAIRS1 // 2 - 1) as i:
                attn_stage((i * 2 + 2, i + 1), 0, i * 2 + 1, 1)
                attn_stage((i * 2 + 3, i + 1), 1, i * 2 + 2, 0)
            attn_stage(None, None, PAIRS1 - 1, 1)

            outputs(0, U_OUT1, 1, DC, M1H, M1L, ready_m1, started=True)
            mean_of_sum(1)
            ffn(0, U_FFN1, ready_h_and_mean(1, 2))
            pe.wait_ge(s_gate, FC)
            outputs(1, U_DOWN1, 2, HALF, MH, ML, lambda k: pe.wait_ge(s_m, M_BASE[1] + k + 1))
            mean_of_sum(3)

            def head_mean(h):
                pe.wait_ge(r_acc, h * 3 + 3)
                pe.matmul(B[7][:], MEAN[:], ACC[:], start=True, stop=True).then_inc(r_mean, 1)

            def ret_head(h, first):
                def unit(n):
                    return Unit(U_RET + n, h, RET_UNITS)

                def project(n, bank):
                    use_unit(pe, unit(n), B[bank][:], DC, HH, HL)

                def project_v(n):
                    u = unit(n)
                    pe.wait_ge(s_hi, u.index + 1)
                    pe.wait_ge(s_lo, u.index + 1)
                    for k in range(2):
                        c = 2 * n + k
                        if first:
                            ready_v(c)
                        wh, wl = (w[u.s][:, RET_VT * k:RET_VT * (k + 1), :] for w in (WH, WL))
                        for tb in range(TB):
                            xh, xl = (x[:, c, P * tb:P * tb + P] for x in (HH, HL))
                            pe.matmul(B[tb][:], xh, wh, start=(c == 0), stop=False)
                            mm = pe.matmul(B[tb][:], xl, wh, start=False, stop=False)
                            if k == 1 and tb == TB - 1:
                                mm.then_inc(s_hi_used, 1)
                            mm = pe.matmul(B[tb][:], xh, wl, start=False, stop=(c == DC - 1))
                    mm.then_inc(s_unit, 1)

                def values(d, bank):
                    for sb_ in range(TB):
                        mm = pe.matmul(B[bank][:, P * sb_:T], VT2[:, sb_, P * d:P * d + P],
                                       SC2[:, T_AT[sb_]:T_AT[sb_] + t_width(sb_)], start=(sb_ == 0),
                                       stop=(sb_ == TB - 1))
                    mm.then_inc(r_pv, 1)

                if first:
                    ready_v = ready_h_and_mean(2, 4)
                else:
                    pe.wait_ge(r_sq, h * RET_VT - 3)
                    pe.wait_ge(r_g, h * RET_VT)
                for n in range(RET_VT):
                    project_v(n)
                    if n == 0 and not first:
                        head_mean(h - 1)
                if not first:
                    pe.wait_ge(r_sq, h * RET_VT)
                project(4, 4)
                if first:
                    pe.wait_ge(s_rb, 4 + 1)
                    for tb in range(TB):
                        mm = pe.transpose(B[7][:, P * tb:P * tb + P], RB[:, P * tb:P * tb + P], IDENT[:])
                    mm.then_inc(r_turned, 1)
                project(5, 5)
                project(6, 6)
                pe.wait_ge(r_v, h * TB + 1)
                project(7, 0)
                pe.wait_ge(r_v, h * TB + 2)
                project(8, 1)
                pe.wait_ge(r_v, h * TB + 3)
                project(9, 2)
                pe.wait_ge(r_qk, h * 4 + 4)
                for sb_, bank, at in ((0, 4, 0), (1, 5, 0), (3, 5, 384), (2, 6, 0)):
                    w = t_width(sb_)
                    for c in range(RET_QT):
                        mm = pe.matmul(B[bank][:, at:at + w], KT2[:, c, P * sb_:P * sb_ + P], QT2[:, c, P * sb_:T],
                                       start=(c == 0), stop=(c == RET_QT - 1))
                    mm.then_inc(r_sc, 1)
                pe.wait_ge(r_v, h * TB + 4)
                project(10, 3)
                pe.wait_ge(r_g, h * RET_VT + 1)
                project(11, 1)
                pe.wait_ge(r_w, h * TB + 4)
                for d, bank in enumerate(SUM_BANKS):
                    values(d, bank)

            pe.wait_ge(s_taken, 8 * 2)
            ret_head(0, True)
            with pe.Fori(1, RET_H) as h:
                ret_head(h, False)

            pe.wait_ge(r_sq, RET_H * RET_VT - 3)
            pe.wait_ge(r_g, RET_H * RET_VT)

            def ready_m2(k):
                if k == 2:
                    head_mean(RET_H - 1)
                pe.wait_ge(s_m, M_BASE[2] + k + 1)
            outputs(2, U_RETO, 2, DC, M2H, M2L, ready_m2)
            pe.wait_ge(s_taken, 8 * 3 - 1)
            ffn(1, U_FFN2, ready_h(3), n=5)
            pe.wait_ge(s_gate, 2 * FC)
            outputs(3, U_DOWN2, 2, HALF, MH, ML, lambda k: pe.wait_ge(s_m, M_BASE[3] + k + 1))

            def ready_m3(k):
                pe.wait_ge(s_m, M_BASE[4] + k + 1)

            def start_out(b):
                if b == 0:
                    pe.wait_ge(b_vs, PAIRS3)
                else:
                    pe.wait_ge(b_v, 2 * PAIRS3)
                start_unit(pe, Unit(U_OUT3 + b), B[b][:], DC, M3H, M3L, ready_m3)

            def stick_stage(j, jp, a, ap):
                u = None if j is None else Unit(U_SB + 3 * jp, j[1], 6)
                jj = None if j is None else j[0]
                first = isinstance(jj, int) and jj == 0

                def z(h):
                    hd = a * 2 + h
                    pe.wait_ge(b_qk, a * 2 + 2)
                    if not (isinstance(a, int) and a * 2 + h == 0):
                        pe.wait_ge(b_zs, hd * 4)
                        if h == 0:
                            pe.wait_ge(b_arg, hd * 3)
                    r = slice(64 * h, 64 * h + 64)
                    for sb_, bank, at in ((0, 2, 0), (1, 3, 0), (3, 3, 384), (2, 4, 0)):
                        w = t_width(sb_)
                        mm = pe.matmul(B[bank][:, at:at + w], KT3[r, ap, P * sb_:P * sb_ + P],
                                       QT3[r, ap, P * sb_:T], start=True, stop=True)
                        mm.then_inc(b_z, 1)

                def later(h):
                    hd = a * 2 + h
                    pe.wait_ge(b_lo, hd + 1)
                    if h == 0:
                        pe.wait_ge(b_zs, hd * 4 + 8)
                    else:
                        pe.wait_ge(b_arg, hd * 3)
                    for sb_, bank, at in ((0, 2, 0), (1, 3, 0), (3, 3, 384), (2, 4, 0)):
                        w = t_width(sb_)
                        for n, part in enumerate((SPH, SPL)):
                            mm = pe.matmul(B[bank][:, at:at + w], LATER[:], part[:, h, T_AT[sb_]:T_AT[sb_] + w],
                                           start=(n == 0 and sb_ != 3), stop=(n == 1 and sb_ == TB - 1),
                                           skip_group_check=True)
                        for s2 in range(sb_ + 1, TB):
                            w2 = t_width(s2)
                            o = at + P * (s2 - sb_)
                            for n, part in enumerate((SPH, SPL)):
                                mm = pe.matmul(B[bank][:, o:o + w2], ALL[:], part[:, h, T_AT[s2]:T_AT[s2] + w2],
                                               start=False, stop=(n == 1 and s2 == TB - 1 and sb_ != 1),
                                               skip_group_check=True)
                        if sb_ != 1:
                            mm.then_inc(b_later, 1)

                def values(h, a, ap):
                    hd = a * 2 + h
                    pe.wait_ge(b_w, hd + 1)
                    if h == 0:
                        pe.wait_ge(b_v, a * 2 + 2)
                        if not (isinstance(a, int) and a == 0):
                            pe.wait_ge(s_m, a + M_BASE[4])
                    for sb_ in range(TB):
                        w = t_width(sb_)
                        mm = pe.matmul(B[7][:, P * sb_:T], VZ3[:, ap, h, sb_, :],
                                       ZS[:, h, T_AT[sb_]:T_AT[sb_] + w], start=(h == 0 and sb_ == 0),
                                       stop=(h == 1 and sb_ == TB - 1), skip_group_check=True)
                    mm.then_inc(b_pv, 1)

                def head_mean(n):
                    pe.wait_ge(b_sq, jj * 2 + n + 1)
                    if first:
                        pe.wait_ge(b_tri, 2)
                    else:
                        pe.wait_ge(b_rq, jj * 2 + n - 1)
                    pe.matmul(B[5 + n][:], HEADMEAN[:], SQ[n][:], start=True, stop=True).then_inc(b_mean, 1)

                if a is not None:
                    z(0)
                if j is not None:
                    if not first:
                        pe.wait_ge(b_vs, jj)
                        use_unit(pe, u, B[0][:], DC, HH, HL)
                    else:
                        pe.wait_ge(s_taken, 8 * 4 - 1)
                        use_unit(pe, u, B[0][:], DC, HH, HL, before=ready_h(4))
                        mean_of_sum(6)
                if a is not None:
                    if not (isinstance(a, int) and a == 0):
                        values(1, a - 1, 1 - ap)
                    z(1)
                    if j is None:
                        start_out(0)
                if j is not None:
                    if not first:
                        pe.wait_ge(b_v, jj * 2)
                    use_unit(pe, u + 1, B[1][:], DC, HH, HL)
                    head_mean(0)
                if a is not None:
                    later(0)
                if j is not None:
                    pe.wait_ge(b_qs, jj * 2 + 1)
                    use_unit(pe, u + 2, B[0][:], DC, HH, HL)
                    head_mean(1)
                if a is not None:
                    if j is None:
                        start_out(1)
                    later(1)
                if j is not None:
                    pe.wait_ge(b_vs, jj + 1)
                    pe.wait_ge(b_qs, jj * 2 + 2)
                    for tb in range(TB):
                        mm = pe.transpose(B[1][:, P * tb:P * tb + P], V3[:, P * tb:P * tb + P], IDENT[:])
                    mm.then_inc(b_vt, 1)
                if a is not None:
                    values(0, a, ap)
                    if j is None:
                        values(1, a, ap)

            stick_stage((0, 0), 0, None, None)
            stick_stage((1, 0), 1, 0, 0)
            with pe.Fori(0, PAIRS3 // 2 - 1) as i:
                stick_stage((i * 2 + 2, i + 1), 0, i * 2 + 1, 1)
                stick_stage((i * 2 + 3, i + 1), 1, i * 2 + 2, 0)
            stick_stage(None, None, PAIRS3 - 1, 1)

            outputs(4, U_OUT3, 1, DC, M3H, M3L, ready_m3, started=True)
            pe.wait_ge(s_taken, 8 * 5 - 1)
            ffn(2, U_FFN3, ready_h(5), n=7)
            pe.wait_ge(s_gate, 3 * FC)
            outputs(5, U_DOWN3, 2, HALF, MH, ML, lambda k: pe.wait_ge(s_m, M_BASE[5] + k + 1))

        @block.scalar
        def _(act):
            EPSC = GAINS[:, G_EPS:G_EPS + 1]

            def square(n, c, b, src):
                if not (n == 0 and isinstance(c, int) and c < 2):
                    act.wait_ge(s_sq_used, c + (8 * n - 1))
                act.activation(SQ[b][:], src, ACT.Square).then_inc(s_squared, 1)

            def input_hi(c, g):
                act.activation(HH[:, c, :], X[:, c, :], ACT.Copy, scale=gain(g, c)).then_inc(s_h_hi, 1)

            def root(n, direct=False):
                if direct:
                    act.wait_ge(s_sq_used, 8 * n + 8)
                else:
                    act.wait_ge(s_mean, SUMS[n])
                act.activation(ACC[:], B[7][:], ACT.Ln, bias=EPSC).then_inc(s_root, 1)
                act.wait_ge(s_root, n + 1)
                act.activation(RB[:], ACC[:], ACT.Exp, scale=-0.5).then_inc(s_rb, 1)

            def ffn(f, u0, chunks_after):
                def pair(i, chunks):
                    split_hi(act, Unit(u0 + 2, i, 2), chunks)
                    act.wait_ge(s_gate, i + (FC * f + 1))
                    act.activation(SG[:], G1[:], ACT.Silu).then_inc(s_silu, 1)
                    split_hi(act, Unit(u0 + 3, i, 2), chunks)
                    act.wait_ge(s_hidden, i + (FC * f + 1))
                    act.copy(MH[:, i, :], HD[:]).then_inc(s_m_hi, 1)
                act.preload_act_table(ACT.Silu)
                with act.Fori(0, FC - 1) as i:
                    pair(i, DC)
                pair(FC - 1, chunks_after)

            def outputs(o, n, u0, per, chunks, chunks_after, gain_post=None, gain_next=None):
                def two(i, after):
                    for b in range(2):
                        c = i * 2 + b
                        for q in range(per):
                            split_hi(act, Unit(u0 + per * b + q + 2, i, 2 * per),
                                     after if per * b + q + 2 >= 2 * per else chunks)
                        if gain_post is not None:
                            act.wait_ge(s_unit, Unit(u0 + per * b + per - 1, i, 2 * per).index + 1)
                            square(n, c, b, B[b][:])
                            act.activation(F[:, c, :], B[b][:], ACT.Copy, scale=gain(gain_post, c))\
                               .then_inc(s_taken, 1)
                        elif gain_next is not None:
                            act.wait_ge(s_taken, c + (8 * o + 1))
                            square(n, c, b, X[:, c, :])
                            input_hi(c, gain_next)
                act.preload_act_table_set(LOG_EXP)
                with act.Fori(0, DC // 2 - 1) as i:
                    two(i, chunks)
                two(DC // 2 - 1, chunks_after)

            def after_post(n, g, updated, split=None):
                for c in range(DC):
                    act.wait_ge(s_x_new, updated + c + 1)
                    square(n, c, c % 2, X[:, c, :])
                    input_hi(c, g)
                    if split is not None and c in (4, 6):
                        split_hi(act, split + (c - 4) // 2, DC)

            for g in range(X_PARTS):
                act.dma_start(X[:, 2 * g:2 * g + 2, :], ins["x_t"][:, 2 * g:2 * g + 2, :]).then_inc(s_x_in[g], 16)
                if g == 0:
                    act.preload_act_table_set(LOG_EXP)
            act.wait_ge(s_gains, 16)
            for c in range(DC):
                act.wait_ge(s_x_in[c // 2], 16)
                square(0, c, c % 2, X[:, c, :])
                input_hi(c, G_MIX1)
                if c == 0:
                    split_hi(act, Unit(0), DC)
            split_hi(act, Unit(1), DC)
            root(0)
            split_hi(act, Unit(2), DC)
            split_hi(act, Unit(3), DC)

            def attn_stage(j, jp, a, ap):
                u = None if j is None else Unit(U_ATTN + 3 * jp, j[1], 6)
                jj = None if j is None else j[0]
                first = isinstance(jj, int) and jj == 0

                def mixed_hi(a):
                    act.wait_ge(a_pv, a * 2 + 2)
                    act.copy(M1H[:, a + POOL_TILES, :], B[7][:]).then_inc(s_m_hi, 1)

                def exps(h):
                    hd = a * 2 + h
                    act.wait_ge(a_negmax, hd + 1)
                    for tb in range(TB):
                        p = PR[:, h, S_AT[tb]:S_AT[tb] + s_width(tb)]
                        act.activation(p, p, ACT.Exp, bias=NM[:, h, tb:tb + 1], scale=0.125,
                                       accum_out=DEN[:, h, tb:tb + 1]).then_inc(a_exp, 1)

                def copy_qk(n):
                    act.wait_ge(s_unit, (u + n).index + 1)
                    if not first:
                        act.wait_ge(a_qk, jj * 2 + n - 1)
                    act.copy(QC[:, n, :], B[n][:]).then_inc(a_copied, 1)

                def copy_probs(h):
                    hd = a * 2 + h
                    act.wait_ge(a_turned, hd * 3 + 2)
                    if not (isinstance(a, int) and a == 0):
                        act.wait_ge(a_pv, hd - 1)
                    act.copy(PT[:, h, 512:1024], B[6][:]).then_inc(a_pt_act, 1)

                if a is not None:
                    exps(0)
                if j is not None:
                    split_hi(act, u + 2, DC)
                    copy_qk(0)
                if a is not None:
                    if not (isinstance(a, int) and a == 0):
                        mixed_hi(a - 1)
                    copy_probs(0)
                if j is not None:
                    split_hi(act, u + 3, DC)
                    copy_qk(1)
                if a is not None:
                    exps(1)
                if j is not None:
                    split_hi(act, u + 4, DC)
                if a is not None:
                    copy_probs(1)
                if j is not None:
                    act.wait_ge(a_vt, jj + 1)
                    if first:
                        act.wait_ge(a_zero, 1)
                    if not (isinstance(jj, int) and jj < 2):
                        act.wait_ge(a_pv, jj * 2 - 2)
                    for h in range(2):
                        act.copy(VZ1[:, jp, h, :, 64 * h:64 * h + 64],
                                 B[0][:].rearrange("p (t d) -> p t d", t=TB)[:, :, 64 * h:64 * h + 64])\
                           .then_inc(a_v, 1)
                elif a is not None:
                    mixed_hi(a)

            attn_stage((0, 0), 0, None, None)
            for t in range(POOL_TILES):
                act.wait_ge(p_y, t + 1)
                if t:
                    act.wait_ge(p_m, t)
                act.activation(YT[:], B[5 + t][:], ACT.Copy, scale=GAINS[:, G_POOL + t:G_POOL + t + 1])\
                   .then_inc(p_yt, 1)
                act.wait_ge(p_yt, t + 1)
                act.copy(M1H[:, t, :], YT[:]).then_inc(p_hi, 1)
            attn_stage((1, 0), 1, 0, 0)
            with act.Fori(0, PAIRS1 // 2 - 1) as i:
                attn_stage((i * 2 + 2, i + 1), 0, i * 2 + 1, 1)
                attn_stage((i * 2 + 3, i + 1), 1, i * 2 + 2, 0)
            attn_stage(None, None, PAIRS1 - 1, 1)

            outputs(0, 1, U_OUT1, 1, DC, DC, gain_post=G_POST1)
            root(1)
            after_post(2, G_FFN1, 0)
            root(2, direct=True)
            ffn(0, U_FFN1, HALF)
            outputs(1, 3, U_DOWN1, 2, HALF, DC, gain_post=G_POSTF1)
            act.dma_start(CS2[:], ins["cos2"]).then_inc(r_tab, 16)
            act.dma_start(SN2[:], ins["sin2"]).then_inc(r_tab, 16)
            root(3)
            after_post(4, G_MIX2, DC, Unit(U_RET + 2))
            root(4, direct=True)

            def ret_tail(h, splits):
                act.preload_act_table_set(LOG_EXP)
                act.wait_ge(r_mean, h + 1)
                act.activation(ACC[:], B[7][:], ACT.Ln, bias=EPSC, scale=D / (RET_VT * P)).then_inc(r_root, 1)
                act.wait_ge(r_root, h + 1)
                act.activation(ACC[:], ACC[:], ACT.Exp, scale=-0.5).then_inc(r_ro, 1)
                for d in range(RET_VT):
                    if d in (0, 2) and splits is not None:
                        split_hi(act, splits + d // 2, DC)
                    act.wait_ge(r_p, h * RET_VT + d + 1)
                    act.copy(M2H[:, h * RET_VT + d, :], O2[:, d, :]).then_inc(s_m_hi, 1)

            def ret_head(h):
                first = isinstance(h, int) and h == 0

                def unit(n):
                    return Unit(U_RET + n, h, RET_UNITS)

                def copy_v(tb):
                    act.activation(VT2[:, tb, :], B[tb][:], ACT.Copy, scale=RBT[:, tb:tb + 1]).then_inc(r_v, 1)

                def take_values(d, bank):
                    act.wait_ge(r_pv, h * RET_VT + d + 1)
                    act.copy(O2[:, d, :], B[bank][:]).then_inc(r_oc, 1)
                    if d >= 2:
                        act.wait_ge(r_acc, h * 3 + d - 1)
                    elif not (isinstance(h, int) and h == 0):
                        act.wait_ge(r_acc, h * 3)
                    act.activation(SQ[d % 2][:], B[bank][:], ACT.Square).then_inc(r_sq, 1)

                def silu(d):
                    act.wait_ge(r_g, h * RET_VT + d + 1)
                    act.activation(SG2[:, d, :], (TA if d % 2 == 0 else TC)[:], ACT.Silu).then_inc(r_sg, 1)

                if not first:
                    act.wait_ge(r_w, h * TB)
                act.dma_start(DECAY[:], ins["decay"][h]).then_inc(r_dec, 16)
                if not first:
                    ret_tail(h - 1, unit(2))
                for n in range(4, 7):
                    split_hi(act, unit(n), DC)
                if first:
                    act.wait_ge(r_turned, 1)
                    act.copy(RBT[:], B[7][:].rearrange("p (t d) -> p t d", t=TB)[:, :, 0:1]).then_inc(r_rbt, 1)
                    act.wait_ge(r_rbt, 1)
                act.wait_ge(s_unit, unit(3).index + 1)
                for tb in range(TB):
                    copy_v(tb)
                for n in range(7, 12):
                    split_hi(act, unit(n), DC)
                silu(0)
                split_hi(act, unit(12), DC)
                silu(1)
                split_hi(act, unit(13), DC)
                silu(2)
                silu(3)
                for d, bank in enumerate(SUM_BANKS):
                    take_values(d, bank)

            ret_head(0)
            with act.Fori(1, RET_H) as h:
                ret_head(h)
            ret_tail(RET_H - 1, None)

            outputs(2, 5, U_RETO, 2, DC, DC, gain_next=G_FFN2)
            root(5)
            ffn(1, U_FFN2, HALF)
            outputs(3, 6, U_DOWN2, 2, HALF, DC, gain_next=G_MIX3)
            act.dma_start(MASK[:], ins["mask"]).then_inc(b_tab, 16)
            act.dma_start(TRI32[:], ins["tri"]).then_inc(b_tab, 16)
            act.dma_start(HEADMEAN[:], ins["headmean"]).then_inc(b_tab, 16)
            root(6)
            act.wait_ge(b_tab, 48)
            act.copy(LATER[:], TRI32[:, 0:P]).then_inc(b_tri, 1)
            act.copy(ALL[:], TRI32[:, P:2 * P]).then_inc(b_tri, 1)

            def stick_stage(j, jp, a, ap):
                u = None if j is None else Unit(U_SB + 3 * jp, j[1], 6)
                jj = None if j is None else j[0]
                first = isinstance(jj, int) and jj == 0

                def log_term(h):
                    hd = a * 2 + h
                    act.wait_ge(b_na, hd + 1)
                    act.activation(LG[:, h, :], LG[:, h, :], ACT.Exp).then_inc(b_lg, 1)
                    act.wait_ge(b_lg, hd * 2 + 1)
                    act.activation(LG[:, h, :], LG[:, h, :], ACT.Ln, bias=1.0).then_inc(b_lg, 1)

                def softplus_hi(h):
                    hd = a * 2 + h
                    act.wait_ge(b_sp, hd * 2 + 1)
                    if not (isinstance(a, int) and a == 0):
                        act.wait_ge(b_later, hd * 3 - 3)
                    act.copy(SPH[:, h, :], SP[:, h, :]).then_inc(b_hi, 1)

                def weights(h):
                    hd = a * 2 + h
                    act.wait_ge(b_arg, hd * 3 + 3)
                    act.activation(ZS[:, h, :], ZS[:, h, :], ACT.Exp).then_inc(b_w, 1)

                def squares(n):
                    act.wait_ge(b_qs, jj * 2 + n + 1)
                    if not first:
                        act.wait_ge(b_mean, jj * 2 + n - 1)
                    act.activation(SQ[n][:], QS[:, n, :], ACT.Square).then_inc(b_sq, 1)

                def mixed_hi(a):
                    act.wait_ge(b_pv, a * 2 + 2)
                    act.copy(M3H[:, a, :], B[7][:]).then_inc(s_m_hi, 1)

                if a is not None:
                    log_term(0)
                if j is not None:
                    squares(0)
                    split_hi(act, u + 2, DC)
                if a is not None:
                    if j is None:
                        mixed_hi(a - 1)
                    softplus_hi(0)
                    if j is not None and not (isinstance(a, int) and a == 0):
                        mixed_hi(a - 1)
                if j is not None:
                    if a is not None:
                        log_term(1)
                    rn(0, jj, first)
                    squares(1)
                elif a is not None:
                    log_term(1)
                if a is not None:
                    softplus_hi(1)
                if j is not None:
                    split_hi(act, u + 3, DC)
                if a is not None:
                    weights(0)
                if j is not None:
                    rn(1, jj, first)
                    split_hi(act, u + 4, DC)
                if a is not None:
                    weights(1)
                if j is not None:
                    act.wait_ge(b_vt, jj + 1)
                    if first:
                        act.wait_ge(b_zero, 1)
                    if not (isinstance(jj, int) and jj < 2):
                        act.wait_ge(b_pv, jj * 2 - 2)
                    for h in range(2):
                        act.copy(VZ3[:, jp, h, :, 64 * h:64 * h + 64],
                                 B[1][:].rearrange("p (t d) -> p t d", t=TB)[:, :, 64 * h:64 * h + 64])\
                           .then_inc(b_v, 1)
                elif a is not None:
                    mixed_hi(a)

            def rn(n, jj, first):
                act.wait_ge(b_mean, jj * 2 + n + 1)
                if not first:
                    act.wait_ge(b_qk, jj * 2 + n - 1)
                act.activation(RQ[:, n, :], B[5 + n][:], ACT.Ln, bias=EPSC).then_inc(s_act, 1)
                act.wait_ge(s_act, jj * 2 + n + 1)
                act.activation(RQ[:, n, :], RQ[:, n, :], ACT.Exp, scale=-0.5).then_inc(b_rq, 1)

            stick_stage((0, 0), 0, None, None)
            stick_stage((1, 0), 1, 0, 0)
            with act.Fori(0, PAIRS3 // 2 - 1) as i:
                stick_stage((i * 2 + 2, i + 1), 0, i * 2 + 1, 1)
                stick_stage((i * 2 + 3, i + 1), 1, i * 2 + 2, 0)
            stick_stage(None, None, PAIRS3 - 1, 1)

            outputs(4, 7, U_OUT3, 1, DC, DC, gain_next=G_FFN3)
            root(7)
            ffn(2, U_FFN3, HALF)
            outputs(5, None, U_DOWN3, 2, HALF, 0)

        @block.vector
        def _(dve):
            steps = Steps(dve, s_dve)

            def zero_sum(n):
                dve.memset(ACC[:], 0.0).then_inc(s_zeroed, 1)

            def add_square(n, c, b):
                dve.wait_ge(s_squared, c + (8 * n + 1))
                dve.wait_ge(s_zeroed, SUMS[n])
                if not (n == 0 and isinstance(c, int) and c == 0):
                    dve.wait_ge(s_sq_used, c + 8 * n)
                dve.tensor_tensor(ACC[:], ACC[:], SQ[b][:], ALU.add).then_inc(s_sq_used, 1)

            def input_lo(which, c, g):
                dve.wait_ge(s_h_hi, c + (8 * which + 1))
                dve.scalar_tensor_tensor(out=HL[:, c, :], in0=X[:, c, :], scalar=gain(g, c),
                                         in1=HH[:, c, :].bitcast(F32), op0=ALU.mult,
                                         op1=ALU.subtract).then_inc(s_h, 1)

            def rnorm(n):
                dve.wait_ge(s_rb, n + 1)

            def ffn(f, u0):
                with dve.Fori(0, FC) as i:
                    wait_unit(dve, Unit(u0, i, 2))
                    dve.tensor_tensor(G1[:], B[0][:], RB[:], ALU.mult).then_inc(s_gate, 1)
                    wait_unit(dve, Unit(u0 + 1, i, 2))
                    dve.tensor_tensor(U1[:], B[1][:], RB[:], ALU.mult).then_inc(s_up, 1)
                    dve.wait_ge(s_silu, i + (FC * f + 1))
                    dve.wait_ge(s_up, i + (FC * f + 1))
                    dve.tensor_tensor(HD[:], SG[:], U1[:], ALU.mult).then_inc(s_hidden, 1)
                    dve.wait_ge(s_m_hi, i + (M_BASE[[1, 3, 5][f]] + 1))
                    dve.wait_ge(s_hidden, i + (FC * f + 1))
                    dve.tensor_tensor(ML[:, i, :], HD[:], MH[:, i, :].bitcast(F32), ALU.subtract).then_inc(s_m, 1)

            def outputs(o, n, u0, per, post, which=None, g=None):
                def two(i):
                    for b in range(2):
                        c = i * 2 + b
                        if not post:
                            wait_unit(dve, Unit(u0 + per * b + per - 1, i, 2 * per))
                            dve.tensor_tensor(X[:, c, :], X[:, c, :], B[b][:], ALU.add).then_inc(s_taken, 1)
                        if n is not None:
                            add_square(n, c, b)
                        if g is not None:
                            dve.wait_ge(s_taken, c + (8 * o + 1))
                            input_lo(which, c, g)
                if n is not None:
                    zero_sum(n)
                with dve.Fori(0, DC // 2) as i:
                    two(i)

            def after_post(base, which, g):
                for c in range(DC + 1):
                    if c < DC:
                        if c == 0:
                            dve.tensor_tensor(F[:, c, :], F[:, c, :], RB[:], ALU.mult).then_inc(s_f0, 1)
                            dve.wait_ge(s_f0, base // DC + 1)
                        else:
                            dve.wait_ge(s_f, base // DC * (DC - 1) + c)
                        dve.tensor_tensor(X[:, c, :], X[:, c, :], F[:, c, :], ALU.add).then_inc(s_x_new, 1)
                    if c:
                        dve.wait_ge(s_x_new, base + c)
                        input_lo(which, c - 1, g)

            zero_sum(0)
            dve.wait_ge(s_gains, 16)
            for c in range(DC):
                dve.wait_ge(s_x_in[c // 2], 16)
                add_square(0, c, c % 2)
                input_lo(0, c, G_MIX1)
            rnorm(0)

            dve.wait_ge(a_zero, 4)
            dve.wait_ge(s_const, 16 * N_CONST)
            for t in range(POOL_TILES):
                dve.wait_ge(s_unit, t + 1)
                dve.tensor_tensor(UP[:, t, pad:], B[t][:], RB[:], ALU.mult).then_inc(p_u, 1)
            for tab in (CS1, SN1):
                steps.done(dve.tensor_tensor(tab[:], tab[:], RB[:], ALU.mult))
            steps.wait()
            steps.end()

            def attn_project(j, jp):
                jj = j[0]
                u = Unit(U_ATTN + 3 * jp, j[1], 6)

                def rotate(n):
                    dve.wait_ge(a_copied, jj * 2 + n + 1)
                    if not (isinstance(jj, int) and jj * 2 + n == 0):
                        dve.wait_ge(a_qk, jj * 2 + n)
                    steps.done(dve.tensor_tensor(RT[:, 0, :], QC[:, n, :], CS1[:], ALU.mult))
                    yield
                    dve.wait_ge(a_swapped, jj * 2 + n + 1)
                    steps.done(dve.tensor_tensor(RT[:, 1, :], B[n][:], SN1[:], ALU.mult))
                    steps.wait()
                    if not (isinstance(jj, int) and jj < 2):
                        dve.wait_ge(a_scores, jj * 2 - 2)
                    dve.tensor_tensor((QT1, KT1)[n][:, jp, :], RT[:, 0, :], RT[:, 1, :], ALU.add).then_inc(a_qk, 1)
                    yield

                def scale_v():
                    wait_unit(dve, u + 2)
                    if not (isinstance(jj, int) and jj == 0):
                        dve.wait_ge(a_vt, jj)
                    dve.tensor_tensor(V1[:], B[0][:], RB[:], ALU.mult).then_inc(a_vs, 1)
                return rotate, scale_v

            ATT_STEPS, PROJ_STEPS = 2, 4

            def attn_stage(j, jp, a, ap, between=()):
                if a is not None:
                    steps.at(a, ATT_STEPS + PROJ_STEPS)
                between = iter(between)

                def mixed_lo(a):
                    dve.wait_ge(s_m_hi, a + 1)
                    dst = a + POOL_TILES
                    dve.tensor_tensor(M1L[:, dst, :], B[7][:], M1H[:, dst, :].bitcast(F32),
                                      ALU.subtract).then_inc(s_m, 1)

                def mask(h):
                    hd = a * 2 + h
                    dve.wait_ge(a_scores, hd + 1)
                    dve.sem_inc(a_mask_start, 1)
                    for tb, bank, at in ((3, 2, 0), (2, 3, 0), (0, 3, 384), (1, 4, 0)):
                        w = s_width(tb)
                        dve.tensor_tensor_reduce(PR[:, h, S_AT[tb]:S_AT[tb] + w], B[bank][:, at:at + w],
                                                 BIAS[:, T - w:T], 1.0, -3.0e38, ALU.add, ALU.max,
                                                 MX[:, h, tb:tb + 1]).then_inc(a_masked, 1)
                    dve.wait_ge(a_masked, hd * 4 + 4)
                    dve.tensor_scalar(NM[:, h, :], MX[:, h, :], -0.125, None, ALU.mult).then_inc(a_negmax, 1)

                def normalise(h):
                    hd = a * 2 + h
                    dve.wait_ge(a_exp, hd * 4 + 4)
                    steps.done(dve.reciprocal(RD[:, h, :], DEN[:, h, :]))
                    steps.wait()
                    for tb in range(TB):
                        p = PR[:, h, S_AT[tb]:S_AT[tb] + s_width(tb)]
                        dve.tensor_scalar(p, p, RD[:, h, tb:tb + 1], None, ALU.mult).then_inc(a_probs, 1)

                def copy_probs(h):
                    hd = a * 2 + h
                    if not (isinstance(a, int) and a == 0):
                        dve.wait_ge(a_pv, hd - 1)
                    dve.wait_ge(a_turned, hd * 3 + 1)
                    dve.tensor_copy(PT[:, h, 0:512], B[5][:]).then_inc(a_pt_dve, 1)
                    dve.wait_ge(a_turned, hd * 3 + 3)
                    dve.tensor_copy(PT[:, h, 1024:1280], B[4][:, 256:512]).then_inc(a_pt_dve, 1)

                if j is not None:
                    rotate, scale_v = attn_project(j, jp)
                    rq, rk = rotate(0), rotate(1)
                if a is not None:
                    mask(0)
                    normalise(0)
                if j is not None:
                    next(between, lambda: None)()
                    next(rq)
                    next(between, lambda: None)()
                if a is not None:
                    if not (isinstance(a, int) and a == 0):
                        mixed_lo(a - 1)
                    copy_probs(0)
                if j is not None:
                    next(rq)
                if a is not None:
                    mask(1)
                    normalise(1)
                if j is not None:
                    next(rk)
                    next(rk)
                    scale_v()
                if a is not None:
                    copy_probs(1)
                    if j is None:
                        mixed_lo(a)

            PSTEP = sem("pool_steps")
            pn = [0]

            def pstep(ins):
                ins.then_inc(PSTEP, 1)
                pn[0] += 1
                dve.wait_ge(PSTEP, pn[0])

            def doubled(dst, src, by, rows=slice(0, P)):
                pstep(dve.tensor_tensor(dst[rows, pad:], src[rows, pad:], src[rows, pad - by:pad + T - by], ALU.add))

            dve.wait_ge(p_u, 2)
            def pools(t):
                doubled(WA, UP[:, t, :], 1)
                doubled(WB, WA, 2)
                if t:
                    doubled(WA, WB, 4)
                    doubled(WB, WA, 8)
                for r, w in ((slice(0, 64), WA), (slice(64, P), WB)):
                    pstep(dve.tensor_tensor(DF[r, t, :], w[r, pad:], INV[r, t, :], ALU.mult))
                dve.tensor_tensor(DF[:, t, :], DF[:, t, :], UP[:, t, pad:], ALU.subtract).then_inc(p_d, 1)

            attn_stage((0, 0), 0, None, None, between=(lambda: pools(0), lambda: pools(1)))
            steps.end()
            for t in range(POOL_TILES):
                dve.wait_ge(p_hi, t + 1)
                dve.tensor_tensor(M1L[:, t, :], YT[:], M1H[:, t, :].bitcast(F32), ALU.subtract).then_inc(p_m, 1)

            attn_stage((1, 0), 1, 0, 0)
            with dve.Fori(0, PAIRS1 // 2 - 1) as i:
                attn_stage((i * 2 + 2, i + 1), 0, i * 2 + 1, 1)
                attn_stage((i * 2 + 3, i + 1), 1, i * 2 + 2, 0)
            attn_stage(None, None, PAIRS1 - 1, 1)
            steps.end(PAIRS1 * ATT_STEPS + (PAIRS1 - 1) * PROJ_STEPS)

            outputs(0, 1, U_OUT1, 1, True)
            rnorm(1)
            after_post(0, 1, G_FFN1)
            rnorm(2)
            ffn(0, U_FFN1)
            outputs(1, 3, U_DOWN1, 2, True)
            rnorm(3)
            after_post(DC, 2, G_MIX2)
            rnorm(4)

            dve.wait_ge(r_tab, 32)
            dve.tensor_tensor(CS2[:], CS2[:], RB[:], ALU.mult).then_inc(r_cs, 1)
            dve.tensor_tensor(SN2[:], SN2[:], RB[:], ALU.mult).then_inc(r_cs, 1)
            dve.wait_ge(r_cs, 2)
            RET_STEPS = 2 * 3 + RET_VT

            def ret_tail(h):
                dve.wait_ge(r_ro, h + 1)
                for d in range(RET_VT):
                    dve.wait_ge(r_oc, h * RET_VT + d + 1)
                    steps.done(dve.scalar_tensor_tensor(out=O2[:, d, :], in0=O2[:, d, :],
                                                        scalar=gain(G_RET, h * RET_VT + d), in1=ACC[:],
                                                        op0=ALU.mult, op1=ALU.mult))
                    dve.wait_ge(r_sg, h * RET_VT + d + 1)
                    steps.wait()
                    dve.tensor_tensor(O2[:, d, :], O2[:, d, :], SG2[:, d, :], ALU.mult).then_inc(r_p, 1)
                    if d:
                        lo(h, d - 1)
                lo(h, RET_VT - 1)

            def ret_head(h):
                first = isinstance(h, int) and h == 0
                steps.at(h, RET_STEPS, 0 if first else RET_VT)

                def unit(n):
                    return Unit(U_RET + n, h, RET_UNITS)

                def rotate(n, dst):
                    x1, x2 = (B[b][:] for b in ((4, 5), (6, 0))[n])
                    wait_unit(dve, unit(4 + 2 * n))
                    steps.done(dve.tensor_tensor(TA[:], x1, CS2[:], ALU.mult))
                    steps.done(dve.tensor_tensor(dst[:, 1, :], x1, SN2[:], ALU.mult))
                    wait_unit(dve, unit(5 + 2 * n))
                    steps.done(dve.tensor_tensor(TC[:], x2, SN2[:], ALU.mult))
                    steps.wait()
                    dve.tensor_tensor(dst[:, 0, :], TA[:], TC[:], ALU.subtract).then_inc(r_qk, 1)
                    dve.wait_ge(r_qk, h * 4 + 2 * n + 1)
                    dve.tensor_tensor(TA[:], x2, CS2[:], ALU.mult).then_inc(r_taken, 2)
                    dve.wait_ge(r_taken, h * TAKEN + (2 * n + 2))
                    dve.tensor_tensor(dst[:, 1, :], dst[:, 1, :], TA[:], ALU.add).then_inc(r_qk, 1)
                    dve.wait_ge(r_qk, h * 4 + 2 * n + 2)

                def scale(n, bank, dst, done):
                    wait_unit(dve, unit(n))
                    dve.tensor_tensor(dst[:], B[bank][:], RB[:], ALU.mult).then_inc(done, 1)

                def add_squares(d):
                    dve.wait_ge(r_sq, h * RET_VT + d + 1)
                    if d == 1:
                        dve.tensor_tensor(ACC[:], SQ[0][:], SQ[1][:], ALU.add).then_inc(r_acc, 1)
                    else:
                        dve.wait_ge(r_acc, h * 3 + d - 1)
                        dve.tensor_tensor(ACC[:], ACC[:], SQ[d % 2][:], ALU.add).then_inc(r_acc, 1)

                if not first:
                    ret_tail(h - 1)
                rotate(0, QT2)
                rotate(1, KT2)
                scale(8, 1, TA, r_g)
                scale(9, 2, TC, r_g)
                dve.wait_ge(r_dec, h * 16 + 16)
                if not first:
                    dve.wait_ge(r_pv, h * RET_VT)
                for n, (sb_, bank, at) in enumerate(((0, 4, 0), (1, 5, 0), (3, 5, 384), (2, 6, 0))):
                    w = t_width(sb_)
                    dve.wait_ge(r_sc, h * TB + (4 if n else 1))
                    dve.tensor_tensor(SC2[:, T_AT[sb_]:T_AT[sb_] + w], B[bank][:, at:at + w], DECAY[:, 0:w],
                                      ALU.mult).then_inc(r_w, 1)
                dve.wait_ge(r_sg, h * RET_VT + 1)
                scale(10, 3, TA, r_g)
                dve.wait_ge(r_sg, h * RET_VT + 2)
                scale(11, 1, TC, r_g)
                for d in range(1, RET_VT):
                    add_squares(d)

            def lo(h, d):
                t = h * RET_VT + d
                dve.wait_ge(s_m_hi, t + (M_BASE[2] + 1))
                dve.wait_ge(r_p, t + 1)
                dve.tensor_tensor(M2L[:, t, :], O2[:, d, :], M2H[:, t, :].bitcast(F32), ALU.subtract).then_inc(s_m, 1)

            ret_head(0)
            with dve.Fori(1, RET_H) as h:
                ret_head(h)
            steps.at(RET_H, RET_STEPS, RET_VT)
            ret_tail(RET_H - 1)
            steps.end(RET_H * RET_STEPS)

            outputs(2, 5, U_RETO, 2, False, 3, G_FFN2)
            rnorm(5)
            ffn(1, U_FFN2)
            outputs(3, 6, U_DOWN2, 2, False, 4, G_MIX3)
            rnorm(6)

            def stick_stage(j, jp, a, ap):
                u = None if j is None else Unit(U_SB + 3 * jp, j[1], 6)
                jj = None if j is None else j[0]
                first = isinstance(jj, int) and jj == 0

                def take_z(h):
                    hd = a * 2 + h
                    if not (isinstance(a, int) and a == 0):
                        dve.wait_ge(b_pv, hd - 1)
                    for n, (sb_, bank, at) in enumerate(((0, 2, 0), (1, 3, 0), (3, 3, 384), (2, 4, 0))):
                        w = t_width(sb_)
                        dve.wait_ge(b_z, hd * 4 + (4 if n else 1))
                        dve.scalar_tensor_tensor(out=ZS[:, h, T_AT[sb_]:T_AT[sb_] + w], in0=B[bank][:, at:at + w],
                                                 scalar=0.125, in1=MASK[:, 0:w], op0=ALU.mult,
                                                 op1=ALU.add).then_inc(b_zs, 1)
                    dve.wait_ge(b_zs, hd * 4 + 4)
                    dve.scalar_tensor_tensor(out=LG[:, h, :], in0=ZS[:, h, :], scalar=-1.0, in1=ZS[:, h, :],
                                             op0=ALU.mult, op1=ALU.min).then_inc(b_na, 1)

                def softplus(h):
                    hd = a * 2 + h
                    dve.wait_ge(b_lg, hd * 2 + 2)
                    dve.scalar_tensor_tensor(out=SP[:, h, :], in0=ZS[:, h, :], scalar=0.0, in1=LG[:, h, :],
                                             op0=ALU.max, op1=ALU.add).then_inc(b_sp, 1)
                    dve.scalar_tensor_tensor(out=ZS[:, h, :], in0=ZS[:, h, :], scalar=0.0, in1=LG[:, h, :],
                                             op0=ALU.min, op1=ALU.subtract).then_inc(b_sp, 1)

                def softplus_lo(h):
                    hd = a * 2 + h
                    dve.wait_ge(b_hi, hd + 1)
                    dve.tensor_tensor(SPL[:, h, :], SP[:, h, :], SPH[:, h, :].bitcast(F32),
                                      ALU.subtract).then_inc(b_lo, 1)

                def exponent(h):
                    hd = a * 2 + h
                    dve.wait_ge(b_sp, hd * 2 + 2)
                    for n, (bank, at, w) in enumerate(((2, 0, 512), (3, 512, 512), (4, 1024, 256))):
                        dve.wait_ge(b_later, hd * 3 + n + 1)
                        dve.tensor_tensor(ZS[:, h, at:at + w], ZS[:, h, at:at + w], B[bank][:, 0:w],
                                          ALU.subtract).then_inc(b_arg, 1)

                def mixed_lo(a):
                    dve.wait_ge(s_m_hi, a + (M_BASE[4] + 1))
                    dve.tensor_tensor(M3L[:, a, :], B[7][:], M3H[:, a, :].bitcast(F32), ALU.subtract).then_inc(s_m, 1)

                def scale_qk(n):
                    wait_unit(dve, u + n)
                    if not first:
                        dve.wait_ge(b_qk, jj * 2 + n - 1)
                    dve.tensor_tensor(QS[:, n, :], B[n][:], RB[:], ALU.mult).then_inc(b_qs, 1)

                def norm_qk(n):
                    dve.wait_ge(b_rq, jj * 2 + n + 1)
                    dve.wait_ge(b_qs, jj * 2 + n + 1)
                    if not (isinstance(jj, int) and jj < 2):
                        dve.wait_ge(b_z, jj * 8 - 8)
                    dve.scalar_tensor_tensor(out=(QT3, KT3)[n][:, jp, :], in0=QS[:, n, :],
                                             scalar=GAINS[:, G_Q + n:G_Q + n + 1], in1=RQ[:, n, :], op0=ALU.mult,
                                             op1=ALU.mult).then_inc(b_qk, 1)

                if a is not None:
                    take_z(0)
                if j is not None:
                    scale_qk(0)
                if a is not None:
                    if j is None:
                        mixed_lo(a - 1)
                    softplus(0)
                    softplus_lo(0)
                    if j is not None and not (isinstance(a, int) and a == 0):
                        mixed_lo(a - 1)
                    take_z(1)
                if j is not None:
                    scale_qk(1)
                if a is not None:
                    softplus(1)
                    exponent(0)
                    softplus_lo(1)
                if j is not None:
                    norm_qk(0)
                    wait_unit(dve, u + 2)
                    if not first:
                        dve.wait_ge(b_vt, jj)
                    dve.tensor_tensor(V3[:], B[0][:], RB[:], ALU.mult).then_inc(b_vs, 1)
                    norm_qk(1)
                if a is not None:
                    exponent(1)
                    if j is None:
                        mixed_lo(a)

            stick_stage((0, 0), 0, None, None)
            dve.wait_ge(b_tab, 48)
            stick_stage((1, 0), 1, 0, 0)
            with dve.Fori(0, PAIRS3 // 2 - 1) as i:
                stick_stage((i * 2 + 2, i + 1), 0, i * 2 + 1, 1)
                stick_stage((i * 2 + 3, i + 1), 1, i * 2 + 2, 0)
            stick_stage(None, None, PAIRS3 - 1, 1)

            outputs(4, 7, U_OUT3, 1, False, 5, G_FFN3)
            rnorm(7)
            ffn(2, U_FFN3)
            outputs(5, None, U_DOWN3, 2, False)


def tables():
    p, t = np.arange(P)[:, None], np.arange(T)[None, :]
    out = {"ident": np.eye(P), "mean": np.full((P, P), 1.0 / D)}

    swap = np.zeros((P, P))
    for m in range(P):
        swap[m ^ 32, m] = 1.0 if m & 32 else -1.0
    out["swap"] = swap

    def angles(half, index):
        freqs = np.power(np.float32(10000.0), (-(np.arange(half) / half)).astype(np.float32)).astype(np.float32)
        return (t.astype(np.float32) * freqs[index]).astype(np.float32).astype(np.float64)
    a1 = angles(32, p % 32)
    out["cos1"], out["sin1"] = np.cos(a1), np.sin(a1)
    a2 = angles(P, p)
    out["cos2"], out["sin2"] = np.cos(a2), np.sin(a2)

    dist = T - P + p - t
    branches = ((dist >= 0) & (dist <= P)).astype(int)
    for dilation in (4, 16):
        branches += (dist >= 0) & (dist % dilation == 0)
    out["bias"] = np.where(branches > 0, 8.0 * np.log(np.maximum(branches, 1)), -1e30)

    gamma = 1.0 - 2.0 ** (-5.0 - np.arange(RET_H))
    seen = (t // 64) >= (p // 64)
    out["decay"] = np.stack([np.where(seen, g ** np.abs(t - p) / 16.0, 0.0) for g in gamma])
    out["mask"] = np.where(t > p, 0.0, -1e30)
    q = np.arange(P)[None, :]
    out["tri"] = np.concatenate([(p > q).astype(float), np.ones((P, P))], axis=1)
    out["headmean"] = np.where(p // 64 == q // 64, 1.0 / 64, 0.0)

    windows = np.array([[2, 8], [4, 16]])
    out["inv_counts"] = np.stack([1.0 / np.minimum(t + 1, windows[p // 64, n]) for n in range(POOL_TILES)], axis=1)
    return {k: np.ascontiguousarray(v, np.float32) for k, v in out.items()}


def unit_tiles(w):
    k, n = w.shape
    return w.reshape(k // P, P, n // P, P).transpose(2, 1, 0, 3)


def halves(tiles):
    n, _, k, _ = tiles.shape
    return tiles.reshape(n, P, 2, k // 2, P).transpose(0, 2, 1, 3, 4).reshape(2 * n, P, k // 2, P)


def interleaved(*parts):
    return np.stack(parts, axis=1).reshape(-1, *parts[0].shape[1:])


def layout(i):
    w_in = unit_tiles(i["w_in"][0])
    q, k, v = (w_in[POOL_TILES + PAIRS1 * n:POOL_TILES + PAIRS1 * (n + 1)] for n in range(3))
    ret = unit_tiles(i["ret_w_in_2"][0])
    nq, nv = RET_H * RET_QT, RET_H * RET_VT
    ret_parts = []
    for h in range(RET_H):
        tiles = ret[2 * nq + RET_VT * h:2 * nq + RET_VT * (h + 1)]
        ret_parts.append(tiles.reshape(RET_VT, P, DC // 2, 2, P).transpose(2, 1, 3, 0, 4).reshape(-1, P, DC, P))
        for base, per in ((0, RET_QT), (nq, RET_QT), (2 * nq + nv, RET_VT)):
            ret_parts.append(ret[base + per * h:base + per * (h + 1)])
    sb = unit_tiles(i["sb_w_in_2"][0])
    ffn = [unit_tiles(i["ffn_w_in_2"][n]) for n in range(2)]
    small = [
        w_in[:POOL_TILES], interleaved(q, k, v), unit_tiles(i["w_out"][0]),
        interleaved(unit_tiles(i["w_gate"][0]), unit_tiles(i["w_up"][0])),
        *ret_parts, halves(unit_tiles(i["ret_w_o_2"][0])), interleaved(ffn[0][:FC], ffn[0][FC:]),
        interleaved(*(sb[PAIRS3 * n:PAIRS3 * (n + 1)] for n in range(3))), unit_tiles(i["sb_w_o_2"][0]),
        interleaved(ffn[1][:FC], ffn[1][FC:]),
    ]
    large = [halves(unit_tiles(w)) for w in (i["w_down"][0], i["ffn_w_out_2"][0], i["ffn_w_out_2"][1])]
    cols = [i[n].reshape(DC, P).T for n in ("ln_pre_mix", "ln_post_mix", "ln_pre_ffn", "ln_post_ffn")]
    for n in range(2):
        cols += [i["mix_norm_2"][n].reshape(DC, P).T, i["ffn_norm_2"][n].reshape(DC, P).T]
    cols.append(i["pool_scale"][0].reshape(POOL_TILES, P).T)
    cols.append(i["ret_out_norm_2"][0].reshape(RET_H * RET_VT, P).T)
    for n in ("sb_q_norm_2", "sb_k_norm_2"):
        cols.append(np.tile(i[n][0], 2)[:, None])
    cols.append(np.full((P, 1), EPS, np.float32))
    w_pool = np.zeros((P, POOL_TILES, P), np.float32)
    for g in range(2 * POOL_TILES):
        r = slice(64 * (g % 2), 64 * (g % 2) + 64)
        w_pool[r, g // 2, r] = i["w_pool"][0, g]
    return {
        "x_t": i["x"][0].T.reshape(DC, P, T).transpose(1, 0, 2),
        "w_small": np.concatenate(small).reshape(-1, P, DC * P),
        "w_large": np.concatenate(large).reshape(-1, P, HALF * P),
        "gains": np.concatenate(cols, axis=1),
        "w_pool": w_pool,
    }


def kernel(**inputs):
    import concourse.bacc as bacc
    from concourse.bass_utils import run_bass_kernel_spmd

    nc = bacc.Bacc("TRN2", target_bir_lowering=False, num_devices=1)
    arrays = layout({k: np.asarray(v) for k, v in inputs.items()}) | tables()
    arrays = {f"in_{k}": np.ascontiguousarray(v) for k, v in arrays.items()}
    ins = {k.removeprefix("in_"): nc.dram_tensor(k, a.shape, mybir.dt.from_np(a.dtype), kind="ExternalInput").ap()
           for k, a in arrays.items()}
    out_t = nc.dram_tensor("out_t", (P, DC, T), F32, kind="ExternalOutput").ap()
    build(nc, ins, out_t)
    r = run_bass_kernel_spmd(nc, [arrays], core_ids=[0])
    got = np.asarray(r.results[0]["out_t"])
    return np.ascontiguousarray(got.transpose(2, 1, 0).reshape(1, T, D))
```
